# Optimizing a Trainium2 kernel written in Bass

```python
import jax, jax.numpy as jnp
from jax import lax
import numpy as np

D_MODEL = 1024
BATCH = 1
SEQ = 256
DEPTH = 2

D_FF = 2816
FFN_HALF = 0.5
N_HEADS = 8
Q_LORA = 352
KV_LORA = 128
QK_NOPE = 64
QK_ROPE = 32
V_HEAD = 64
ROPE_THETA = 10000.0
Q_BLOCK = 128
CONV_CH = 256
CONV_WIDTH = 31
POOL_WINDOWS = (2, 4, 8, 16)
POOL_GROUPS = 4
POOL_GC = 128
FNET_GROUPS = 4
FNET_GC = 128
N_BRANCH = 4
W_A = Q_LORA + KV_LORA + QK_ROPE
W_B = 2 * CONV_CH
W_C = POOL_GROUPS * POOL_GC
W_D = FNET_GROUPS * FNET_GC
W_MIX = W_A + W_B + W_C + W_D
W_IN = W_MIX + N_BRANCH * D_MODEL
N_SUB = 3
N_MOD = 3 * N_SUB
EPS = 1e-6

kernel_name = "hybrid_gated_mla_conv_pool_fnet_encoder"

def rmsnorm(x, g):
    x32 = x.astype(jnp.float32)
    y = x32 * lax.rsqrt(jnp.mean(x32 * x32, axis=-1, keepdims=True) + EPS)
    return (y * g.astype(jnp.float32)).astype(x.dtype)

def layernorm(x, g, b):
    x32 = x.astype(jnp.float32)
    mu = jnp.mean(x32, axis=-1, keepdims=True)
    xc = x32 - mu
    y = xc * lax.rsqrt(jnp.mean(xc * xc, axis=-1, keepdims=True) + EPS)
    return (y * g.astype(jnp.float32) + b.astype(jnp.float32)).astype(x.dtype)

def modulate(h, shift, scale):
    return h * (1 + scale[:, None, :]) + shift[:, None, :]

def swiglu(h, w_in, w_out):
    gu = h @ w_in
    g, u = jnp.split(gu, 2, axis=-1)
    return (jax.nn.silu(g) * u) @ w_out

def rope_tables(seq, dim):
    pos = jnp.arange(seq, dtype=jnp.float32)
    inv = ROPE_THETA ** (-jnp.arange(0, dim, 2, dtype=jnp.float32) / dim)
    ang = pos[:, None] * inv[None, :]
    return jnp.cos(ang), jnp.sin(ang)

def apply_rope(x, cos, sin):
    x1, x2 = jnp.split(x, 2, axis=-1)
    c = cos.astype(x.dtype)
    s = sin.astype(x.dtype)
    return jnp.concatenate([x1 * c - x2 * s, x1 * s + x2 * c], axis=-1)

def dense_attention(q, k, v):
    B, S, H, Dq = q.shape
    nb = S // Q_BLOCK
    qb = q.reshape(B, nb, Q_BLOCK, H, Dq).transpose(1, 0, 2, 3, 4)
    sm_scale = Dq ** -0.5

    def one_block(qblk):
        s = jnp.einsum('bqhd,bkhd->bhqk', qblk, k).astype(jnp.float32) * sm_scale
        p = jax.nn.softmax(s, axis=-1).astype(v.dtype)
        return jnp.einsum('bhqk,bkhd->bqhd', p, v)

    o = lax.map(one_block, qb)
    return o.transpose(1, 0, 2, 3, 4).reshape(B, S, H, v.shape[-1])

def mla_mixer(za, q_norm_g, w_uq, kv_norm_g, w_ukv, w_a):
    B, S, _ = za.shape
    cq = za[..., :Q_LORA]
    ckv = za[..., Q_LORA:Q_LORA + KV_LORA]
    kr = za[..., Q_LORA + KV_LORA:]
    cos, sin = rope_tables(S, QK_ROPE)
    q = (rmsnorm(cq, q_norm_g) @ w_uq).reshape(B, S, N_HEADS, QK_NOPE + QK_ROPE)
    q_nope, q_rope = q[..., :QK_NOPE], q[..., QK_NOPE:]
    q_rope = apply_rope(q_rope, cos[:, None, :], sin[:, None, :])
    kv = (rmsnorm(ckv, kv_norm_g) @ w_ukv).reshape(B, S, N_HEADS, QK_NOPE + V_HEAD)
    k_nope, v = kv[..., :QK_NOPE], kv[..., QK_NOPE:]
    k_rope = apply_rope(kr, cos, sin)
    k_rope = jnp.broadcast_to(k_rope[:, :, None, :], (B, S, N_HEADS, QK_ROPE))
    qf = jnp.concatenate([q_nope, q_rope], axis=-1)
    kf = jnp.concatenate([k_nope, k_rope], axis=-1)
    o = dense_attention(qf, kf, v).reshape(B, S, N_HEADS * V_HEAD)
    return o @ w_a

def conv_mixer(zb, conv_w, conv_b, ln_g, ln_b, w_b):
    a, gt = jnp.split(zb, 2, axis=-1)
    u = a * jax.nn.sigmoid(gt)
    pad = CONV_WIDTH // 2
    y = lax.conv_general_dilated(
        u, conv_w[:, None, :].astype(u.dtype), window_strides=(1,), padding=[(pad, pad)],
        dimension_numbers=('NWC', 'WIO', 'NWC'), feature_group_count=CONV_CH) + conv_b
    y = jax.nn.silu(layernorm(y, ln_g, ln_b))
    return y @ w_b

def pool_mixer(zc, pool_w, pool_scale, w_c):
    B, S, _ = zc.shape
    ug = zc.reshape(B, S, POOL_GROUPS, POOL_GC)
    cs = jnp.cumsum(ug.astype(jnp.float32), axis=1)
    cs = jnp.pad(cs, ((0, 0), (1, 0), (0, 0), (0, 0)))
    t = jnp.arange(S)
    means = []
    for g, w in enumerate(POOL_WINDOWS):
        lo = w // 2
        hi = w - 1 - lo
        start = jnp.clip(t - lo, 0, S)
        end = jnp.clip(t + hi + 1, 0, S)
        win = cs[:, end, g] - cs[:, start, g]
        cnt = (end - start).astype(jnp.float32)[None, :, None]
        means.append(win / cnt)
    mean = jnp.stack(means, axis=2)
    d = (mean - ug.astype(jnp.float32)).astype(zc.dtype)
    y = jnp.einsum('bsgc,gcd->bsgd', d, pool_w).reshape(B, S, W_C) * pool_scale
    return y @ w_c

def fourier_mixer(zd, w_d):
    B, S, _ = zd.shape
    v = zd.astype(jnp.float32).reshape(B, S, FNET_GROUPS, FNET_GC)
    f = jnp.fft.fft2(v, axes=(1, 3), norm='ortho').real
    return f.astype(zd.dtype).reshape(B, S, W_D) @ w_d

def token_mixer(h, w_in, q_norm_g, w_uq, kv_norm_g, w_ukv, w_a, conv_w, conv_b,
                conv_ln_g, conv_ln_b, w_b, pool_w, pool_scale, w_c, w_d, w_out):
    B, S, D = h.shape
    z = h @ w_in
    za = z[..., :W_A]
    zb = z[..., W_A:W_A + W_B]
    zc = z[..., W_A + W_B:W_A + W_B + W_C]
    zd = z[..., W_A + W_B + W_C:W_MIX]
    gates = jax.nn.sigmoid(z[..., W_MIX:]).reshape(B, S, N_BRANCH, D)
    y_a = mla_mixer(za, q_norm_g, w_uq, kv_norm_g, w_ukv, w_a)
    y_b = conv_mixer(zb, conv_w, conv_b, conv_ln_g, conv_ln_b, w_b)
    y_c = pool_mixer(zc, pool_w, pool_scale, w_c)
    y_d = fourier_mixer(zd, w_d)
    merged = (gates[:, :, 0] * y_a + gates[:, :, 1] * y_b
              + gates[:, :, 2] * y_c + gates[:, :, 3] * y_d)
    return merged @ w_out

def setup_inputs(seed: int = 0) -> dict:
    key = jax.random.key(seed)
    ks = jax.random.split(key, 32)
    f32 = jnp.float32
    L, D = DEPTH, D_MODEL

    def nrm(k, shape, scale):
        return jax.random.normal(k, shape, f32) * scale

    return {
        "x": nrm(ks[0], (BATCH, SEQ, D), 1.0),
        "c": nrm(ks[1], (BATCH, D), 1.0),
        "ada_w": nrm(ks[2], (L, D, N_MOD * D), 0.5 * D ** -0.5),
        "ada_b": nrm(ks[3], (L, N_MOD * D), 0.02),
        "norm_g": 1.0 + nrm(ks[4], (L, 2 * N_SUB, D), 0.02),
        "ffn1_w_in": nrm(ks[5], (L, D, 2 * D_FF), D ** -0.5),
        "ffn1_w_out": nrm(ks[6], (L, D_FF, D), D_FF ** -0.5),
        "ffn2_w_in": nrm(ks[7], (L, D, 2 * D_FF), D ** -0.5),
        "ffn2_w_out": nrm(ks[8], (L, D_FF, D), D_FF ** -0.5),
        "w_in": nrm(ks[9], (L, D, W_IN), D ** -0.5),
        "q_norm_g": 1.0 + nrm(ks[10], (L, Q_LORA), 0.02),
        "w_uq": nrm(ks[11], (L, Q_LORA, N_HEADS * (QK_NOPE + QK_ROPE)), Q_LORA ** -0.5),
        "kv_norm_g": 1.0 + nrm(ks[12], (L, KV_LORA), 0.02),
        "w_ukv": nrm(ks[13], (L, KV_LORA, N_HEADS * (QK_NOPE + V_HEAD)), KV_LORA ** -0.5),
        "w_a": nrm(ks[14], (L, N_HEADS * V_HEAD, D), (N_HEADS * V_HEAD) ** -0.5),
        "conv_w": nrm(ks[15], (L, CONV_WIDTH, CONV_CH), CONV_WIDTH ** -0.5),
        "conv_b": nrm(ks[16], (L, CONV_CH), 0.02),
        "conv_ln_g": 1.0 + nrm(ks[17], (L, CONV_CH), 0.02),
        "conv_ln_b": nrm(ks[18], (L, CONV_CH), 0.02),
        "w_b": nrm(ks[19], (L, CONV_CH, D), CONV_CH ** -0.5),
        "pool_w": nrm(ks[20], (L, POOL_GROUPS, POOL_GC, POOL_GC), POOL_GC ** -0.5),
        "pool_scale": 1.0 + nrm(ks[21], (L, W_C), 0.1),
        "w_c": nrm(ks[22], (L, W_C, D), W_C ** -0.5),
        "w_d": nrm(ks[23], (L, W_D, D), W_D ** -0.5),
        "w_out": nrm(ks[24], (L, D, D), D ** -0.5),
    }

def reference(x, c, ada_w, ada_b, norm_g, ffn1_w_in, ffn1_w_out, ffn2_w_in, ffn2_w_out,
              w_in, q_norm_g, w_uq, kv_norm_g, w_ukv, w_a, conv_w, conv_b, conv_ln_g,
              conv_ln_b, w_b, pool_w, pool_scale, w_c, w_d, w_out):
    B = x.shape[0]
    c_act = jax.nn.silu(c)
    for l in range(DEPTH):
        mod = (c_act @ ada_w[l] + ada_b[l]).reshape(B, N_MOD, D_MODEL)
        h = modulate(rmsnorm(x, norm_g[l, 0]), mod[:, 0], mod[:, 1])
        y = rmsnorm(swiglu(h, ffn1_w_in[l], ffn1_w_out[l]), norm_g[l, 1])
        x = x + FFN_HALF * mod[:, 2][:, None, :] * y
        h = modulate(rmsnorm(x, norm_g[l, 2]), mod[:, 3], mod[:, 4])
        y = token_mixer(h, w_in[l], q_norm_g[l], w_uq[l], kv_norm_g[l], w_ukv[l], w_a[l],
                        conv_w[l], conv_b[l], conv_ln_g[l], conv_ln_b[l], w_b[l],
                        pool_w[l], pool_scale[l], w_c[l], w_d[l], w_out[l])
        x = x + mod[:, 5][:, None, :] * rmsnorm(y, norm_g[l, 3])
        h = modulate(rmsnorm(x, norm_g[l, 4]), mod[:, 6], mod[:, 7])
        y = rmsnorm(swiglu(h, ffn2_w_in[l], ffn2_w_out[l]), norm_g[l, 5])
        x = x + FFN_HALF * mod[:, 8][:, None, :] * y
    return x


_drawn_inputs = setup_inputs


def setup_inputs(seed=0):
    import zlib

    import numpy as np

    out = dict(_drawn_inputs(seed))
    spreads = {}
    factors = {'norm_g': 3.615,
     'q_norm_g': 8.0,
     'kv_norm_g': 8.0,
     'conv_b': 8.0,
     'conv_ln_g': 8.0,
     'conv_ln_b': 8.0}
    for name, (base, spread) in spreads.items():
        noise = np.random.default_rng([zlib.crc32(name.encode()), seed]).standard_normal(out[name].shape)
        drawn = base * np.exp(spread * noise) if base else spread * noise
        out[name] = __import__('jax').numpy.asarray(drawn.astype(out[name].dtype))
    for name, factor in factors.items():
        out[name] = (out[name] * factor).astype(out[name].dtype)
    return out
```

```python
import concourse.bass as bass
from concourse import mybir
from contextlib import ExitStack

D = 1024
S = 256
L = 2
FF = 2816
H = 8
QL = 352
KVL = 128
NOPE = 64
ROPE = 32
VH = 64
QKD = NOPE + ROPE
CW = 31
CC = 256
WINDOWS = (2, 4, 8, 16)
EPS = 1e-6
P128 = 128
KD = D // P128
KF = FF // P128
UPW = 256
N_UP = FF // UPW
N_DOWN = 6
MIX = 2048
BAND = 136
BAND0 = 120

FFN_STEPS = N_UP + N_DOWN
MIX_STEPS = 20
PANELS = 2 * FFN_STEPS + MIX_STEPS
STAGE_PANEL = (0, FFN_STEPS, FFN_STEPS + MIX_STEPS)
STAGE_GROUP = (0, 13, 39)
UQ, UKV = 4, 5
BRANCH_STEPS = {3: 6, 2: 9, 1: 12, 0: 15}
ADA_STEPS = 12
MIX_ADA = (0, 1, 2, 3, 9, 11, 12, 13, 14, 15, 16, 17)

FFN_GROUPS_SPLIT = N_UP + 3


def segments(panel):
    if panel < 0:
        panel += PANELS
    for s in (0, 2):
        q = panel - STAGE_PANEL[s]
        if 0 <= q < FFN_STEPS:
            return 2 if q == FFN_GROUPS_SPLIT else 1
    q = panel - STAGE_PANEL[1]
    return 2 if q in (UQ, UKV, 8, 11, 14, 17) else 1


MM_BEFORE = [0]
for _p in range(PANELS):
    MM_BEFORE.append(MM_BEFORE[-1] + 2 * segments(_p))
MM_LAYER = MM_BEFORE[-1]


def build(nc, x, c, ada_w, ada_b, norm_g, ffn1_w_in, ffn1_w_out, ffn2_w_in, ffn2_w_out, w_in,
          q_norm_g, w_uq, kv_norm_g, w_ukv, w_a, conv_w, conv_b, conv_ln_g, conv_ln_b, w_b,
          pool_w, pool_scale, w_c, w_d, w_out, ident_c, dft_c, chan_c, band_c, rope_c, out):
    f32 = mybir.dt.float32
    f32r = mybir.dt.float32r
    ALU = mybir.AluOpType
    ACT = mybir.ActivationFunctionType
    AX = mybir.AxisListType
    ds = bass.ds

    ctx = ExitStack()
    with ctx:
        place = [(nc.sbuf_base + 31) // 32 * 32]

        def at(name, shape, offset, dt=f32):
            return nc.alloc_sbuf_tensor_at(name, shape, dt, offset=offset)

        def sb(name, shape, dt=f32):
            n = 4
            for s in shape[1:]:
                n *= s
            off = place[0]
            place[0] += (n + 31) // 32 * 32
            return at(name, shape, off, dt)

        raw = sb("raw", [128, 2, 4096])
        rings = place[0]
        w_hi = sb("w_hi", [128, 2, 4096], f32r)
        w_lo = sb("w_lo", [128, 2, 4096], f32r)
        ada = sb("ada", [128, 2, 2, 512])
        xs = sb("xs", [128, 2, D])
        hT_hi = sb("hT_hi", [128, KD, S], f32r)
        hT_lo = sb("hT_lo", [128, KD, S], f32r)
        modacc_at = place[0]
        modacc = sb("modacc", [128, 6, 512])
        gain = sb("gain", [128, D])
        tmp = sb("tmp", [128, 2, D])
        dft = sb("dft", [128, 2, 512])
        band = sb("band", [128, 2, 4, BAND])
        chan = sb("chan", [128, 2, 128])
        ident = sb("ident", [128, 128])
        ones = sb("ones", [128, 128])
        rope = sb("rope", [128, 2, 2, 16])
        NV = 110
        NVC = NV + 2 * CW
        vec_all = sb("vec_all", [128, L * NVC])
        vec = sb("vec", [128, NVC])
        poolw = sb("poolw", [128, 4, 128])
        c_raw = sb("c_raw", [128, 8])
        c_act = sb("c_act", [128, 8])
        mods = sb("mods", [128, 16])
        ab = sb("ab", [128, 3, 8])
        minus_half = sb("minus_half", [128, 4])
        ssx = sb("ssx", [128, 2])
        rsx = sb("rsx", [128, 2])
        ssy = sb("ssy", [128, 2, 2])
        rsy = sb("rsy", [128, 2])
        ssa = sb("ssa", [128, 2, 2])
        rsa = sb("rsa", [128, 2, 2])
        k_rot = sb("k_rot", [128, 2, ROPE])
        bns = sb("bns", [128, 2, 6])
        mv = sb("mv", [128, 2, 2])
        rsc = sb("rsc", [128, 2])
        mx = sb("mx", [128, 4])
        nmx = sb("nmx", [128, 4])
        rs = sb("rs", [128, 4])
        rinv = sb("rinv", [128, 4])
        arena = place[0]
        assert arena + 55552 <= nc.sbuf_usable_end, (arena + 55552, nc.sbuf_usable_end)

        hid_hi = at("hid_hi", [128, KF, S], arena, f32r)
        hid_lo = at("hid_lo", [128, KF, S], arena + 22528, f32r)
        hid = at("hid", [128, 2, 2, UPW], arena + 45056)
        junk = at("junk", [128, D], arena + 45056)
        kT = at("kT", [128, H, S], arena)
        U = at("U", [128, 4, 512], arena)
        qT = at("qT", [128, H, S], arena + 8192)
        kf = at("kf", [128, 2, H * QKD], arena + 8192)
        zt = at("zt", [128, 2, 2, 512], arena + 16384)
        gates = at("gates", [128, 2, D], arena + 16384)
        aT_hi = at("aT_hi", [128, 4, S], arena + 24576, f32r)
        za = at("za", [128, 2, 512], arena + 28672)
        bT_hi = at("bT_hi", [128, 4, S], arena + 24576, f32r)
        bT_lo = at("bT_lo", [128, 4, S], arena + 28672, f32r)
        qf = at("qf", [128, 2, H * QKD], arena + 32768)
        oT_hi = at("oT_hi", [128, 4, S], arena + 32768, f32r)
        oT_lo = at("oT_lo", [128, 4, S], arena + 36864, f32r)
        rot = at("rot", [128, 4, 128], arena + 38912)
        dT = at("dT", [128, 4, S], arena + 40960)
        pT = at("pT", [128, 2, 4, 128], arena + 40960)
        aT_lo = at("aT_lo", [128, 4, S], arena + 45056, f32r)
        p = at("p", [128, 4, S], arena + 45056)
        PADW = S + CW - 1
        uT = at("uT", [128, 2, PADW], arena + 49152)
        lnv = at("lnv", [128, 2, S], arena + 49152)
        yc = at("yc", [128, 2, S], arena + 51456)
        lnx = at("lnx", [128, 2, CC], arena + 51456)
        u = at("u", [128, 2, CC], arena + 53504)
        sgv = at("sgv", [128, 2, S], arena + 53504)
        v = at("v", [128, 2, H * VH], modacc_at + 8192)
        pro_ada = [at(f"pro_ada{i}", [128, 2048], arena + 8192 * i if i < 4 else rings + 32768 + 8192 * (i - 4))
                   for i in range(8)]
        rows = at("rows", [128, L, 128], arena + 40960)
        crows = at("crows", [2 * CW, L, 128], arena + 41984)

        Z = [[ctx.enter_context(nc.psum_tensor(f"Z{i}{j}", [128, 512], f32)) for j in range(2)] for i in range(2)]
        T = [ctx.enter_context(nc.psum_tensor(f"T{i}", [128, 512], f32)) for i in range(4)]

        V_G, V_B, V_CB, V_LG, V_LB, V_PS, V_QG, V_KG, V_CW = 0, 24, 96, 98, 100, 102, 106, 109, 110

        class Signal:

            def __init__(self, name, per_layer, credit=0):
                self.sem = ctx.enter_context(nc.semaphore(name))
                self.per_layer, self.credit = per_layer, credit

            def at(self, l, n):
                return l * self.per_layer + n + self.credit

        class Chain(Signal):

            def start(self, eng, l):
                self.eng, self.l, self.n, self.extra = eng, l, 0, 0

            def link(self, ins):
                ins.then_inc(self.sem, 1)
                self.n += 1
                self.eng.wait_ge(self.sem, self.at(self.l, self.n) + self.extra)

        raw_arrived = [Signal(f"raw_arrived{s}", PANELS // 2 * 32) for s in range(2)]
        hi_done = Signal("hi_done", 4 * PANELS)
        lo_done = Signal("lo_done", 4 * PANELS, credit=8)
        mm_done = Signal("mm_done", MM_LAYER, credit=4)
        ada_arrived = [Signal(f"ada_arrived{s}", 3 * ADA_STEPS * 16) for s in range(2)]
        ada_done = Signal("ada_done", 6 * ADA_STEPS, credit=2)
        x_updated = Signal("x_updated", 6, credit=2)
        ssx_ready = Signal("ssx_ready", 6)
        rsx_ready = Signal("rsx_ready", 6)
        xn_ready = Signal("xn_ready", 6)
        ht_filled = Signal("ht_filled", 12)
        hf_act = Signal("hf_act", 6)
        hf_dve = Signal("hf_dve", 6)
        ht_hi = Signal("ht_hi", 12)
        ht_lo = Signal("ht_lo", 12)
        ab_ready = Signal("ab_ready", 3)
        ssy_ready = Signal("ssy_ready", 12)
        y_scaled = Signal("y_scaled", 12)
        rsy_ready = Signal("rsy_ready", 6)
        silu_ready = Signal("silu_ready", 4 * N_UP)
        hid_ready = Signal("hid_ready", 4 * N_UP)
        hid_filled = Signal("hid_filled", 2 * N_UP)
        hid_hi_ready = Signal("hid_hi_ready", 2 * N_UP)
        hid_lo_ready = Signal("hid_lo_ready", 2 * N_UP)
        rows_arrived = Signal("rows_arrived", 96)
        gain_summed = Signal("gain_summed", 6)
        gain_read = Signal("gain_read", 6)
        cols_summed = Signal("cols_summed", 3, credit=1)
        mods_read = Signal("mods_read", 3, credit=1)
        za_copied = Signal("za_copied", 2)
        ssa_ready = Signal("ssa_ready", 2)
        rsa_ready = Signal("rsa_ready", 2)
        an_ready = Signal("an_ready", 2)
        an_filled = Signal("an_filled", 2)
        a_hi = Signal("a_hi", 4)
        a_lo = Signal("a_lo", 4)
        sgb_ready = Signal("sgb_ready", 2)
        u_ready = Signal("u_ready", 2)
        u_filled = Signal("u_filled", 1)
        uT_ready = Signal("uT_ready", 1)
        zt_copied = Signal("zt_copied", 4)
        pool1_done = Signal("pool1_done", 2)
        dT_act = Signal("dT_act", 1)
        dT_dve = Signal("dT_dve", 1)
        pool2_done = Signal("pool2_done", 2)
        fnet1_done = Signal("fnet1_done", 4)
        U_act = Signal("U_act", 2)
        U_dve = Signal("U_dve", 2)
        fnet2_done = Signal("fnet2_done", 2)
        b_hi = Signal("b_hi", 2 + 2 + 1)
        b_lo = Signal("b_lo", 2 + 2 + 1)
        q_copied = Signal("q_copied", 4)
        kv_copied = Signal("kv_copied", 4)
        k_rotated = Signal("k_rotated", 2)
        q_rotated = Signal("q_rotated", 2)
        kq_filled = Signal("kq_filled", 8)
        kq_act = Signal("kq_act", 4)
        kq_dve = Signal("kq_dve", 4)
        scores_done = Signal("scores_done", 8)
        nmx_ready = Signal("nmx_ready", 4)
        exp_done = Signal("exp_done", 4)
        p_ready = Signal("p_ready", 4)
        pT_filled = Signal("pT_filled", 8)
        pT_act = Signal("pT_act", 4)
        pT_dve = Signal("pT_dve", 4)
        o_done = Signal("o_done", 4)
        o_hi = Signal("o_hi", 4)
        o_lo = Signal("o_lo", 4)
        yc_ready = Signal("yc_ready", 1)
        yc_filled = Signal("yc_filled", 1)
        mv_ready = Signal("mv_ready", 1)
        rsc_ready = Signal("rsc_ready", 1)
        lnx_ready = Signal("lnx_ready", 1)
        lnx_filled = Signal("lnx_filled", 1)
        sgv_ready = Signal("sgv_ready", 1)
        lnv_ready = Signal("lnv_ready", 1)
        gate_ready = Signal("gate_ready", 16)
        merged_done = Signal("merged_done", 16)
        m_filled = Signal("m_filled", 4)
        m_hi = Signal("m_hi", 4)
        m_lo = Signal("m_lo", 4)
        vec_ready = Signal("vec_ready", 1)
        poolw_arrived = Signal("poolw_arrived", 16)
        c_arrived = ctx.enter_context(nc.semaphore("c_arrived"))
        x_arrived = ctx.enter_context(nc.semaphore("x_arrived"))
        vrows_arrived = ctx.enter_context(nc.semaphore("vrows_arrived"))
        consts_arrived = ctx.enter_context(nc.semaphore("consts_arrived"))
        pro_arrived = [ctx.enter_context(nc.semaphore(f"pro_arrived{i}")) for i in range(8)]
        set_up = ctx.enter_context(nc.semaphore("set_up"))
        rows_clear = ctx.enter_context(nc.semaphore("rows_clear"))
        c_ready = ctx.enter_context(nc.semaphore("c_ready"))
        pro_done = ctx.enter_context(nc.semaphore("pro_done"))
        pro_filled = ctx.enter_context(nc.semaphore("pro_filled"))
        out_stored = ctx.enter_context(nc.semaphore("out_stored"))
        passed = {e: ctx.enter_context(nc.semaphore(f"passed_{e}")) for e in ("dve", "pool")}

        def pass_waits(eng, e):
            eng.sem_inc(passed[e], 1)

        dve_chain = Chain("dve_chain", 0)
        act_chain = Chain("act_chain", 0)
        pool_chain = Chain("pool_chain", 0)

        def stage_panel(stage, q, i=0):
            b = STAGE_PANEL[stage] + q
            return b + 2 * i, b % 2, b // 2 + i

        def down_blocks(q):
            j = q - N_UP
            return [(b // KF, b % KF) for b in range(max(8 * j - 4, 0), 8 * j + 4)]

        def pieces(stage, q):
            if stage != 1:
                width = 512 if q == N_UP else 1024
            elif q == UQ:
                return [(128, 0, 384), (128, 384, 768), (128, 768, 1536), (QL - 256, 1536, 2304)]
            elif q == UKV:
                width = 256
            else:
                width = 512 if q == BRANCH_STEPS[1] + 2 else 1024
            return [(128, i * width, (i + 1) * width) for i in range(4)]

        def mm_after(panel, seg=None, tok=1):
            if seg is None:
                seg = segments(panel) - 1
            return MM_BEFORE[panel] + 2 * seg + tok + 1

        def mm_group(stage, q, seg=0, tok=1):
            return mm_after(STAGE_PANEL[stage] + q, seg, tok)

        def pair_of(stage, g):
            return (STAGE_GROUP[stage] + g) % 2

        block = ctx.enter_context(nc.Block())

        @block.sync
        def _(sp):
            sp.dma_start(c_raw[:], c.rearrange("b (p j) -> p (b j)", j=8)).then_inc(c_arrived, 16)
            ada_rows = ada_w.rearrange("l (p j) n -> p l j n", j=8)
            for h in range(4):
                for e in range(2):
                    sp.dma_start(pro_ada[2 * h + e][:].rearrange("p (o j n) -> p o j n", o=1, j=4),
                                 ada_rows[:, 0:1, 4 * e:4 * e + 4, 512 * h:512 * h + 512]
                                 ).then_inc(pro_arrived[2 * h + e], 16)

            big = {0: (ffn1_w_in, ffn1_w_out), 2: (ffn2_w_in, ffn2_w_out)}
            kview = lambda w: w.rearrange("l (k p) n -> p l k n", p=128)

            def load_blocks(slot, first, w, l, k0, k1, col, n, parts=128):
                dst = raw[0:parts, slot, first:first + (k1 - k0) * n]
                sp.dma_start(dst.rearrange("p (o k n) -> p o k n", o=1, k=k1 - k0),
                             w[0:parts, ds(l, 1), k0:k1, ds(col, n)]).then_inc(raw_arrived[slot].sem, 16)

            def wait_raw_slot(l, stage, q, i):
                panel, slot, _ = stage_panel(stage, q, i)
                sp.wait_ge(lo_done.sem, lo_done.at(l, 4 * (panel - 1)))
                return slot

            def load_ada(l, stage, q, i):
                half = q // 2 + i
                for e in range(2):
                    sp.wait_ge(ada_done.sem, ada_done.at(l, 2 * (ADA_STEPS * stage + q + 2 * i) + e - 1))
                    j0 = 4 * (q % 2) + 2 * e
                    if stage < 2:
                        lw, col = l, (3 * stage + 2) * D + 512 * half
                        src = ada_rows[:, ds(lw, 1), j0:j0 + 2, ds(col, 512)]
                    elif q < 4:
                        src = ada_rows[:, ds(l, 1), j0:j0 + 2, ds(8 * D + 512 * half, 512)]
                    else:
                        src = ada_rows[:, L - 1:L, j0:j0 + 2, ds(512 * half - 2 * 512, 512)]
                    sp.dma_start(ada[:, e:e + 1, :, :], src).then_inc(ada_arrived[e].sem, 16)

            def load_up(l, stage, q, i=0):
                slot = wait_raw_slot(l, stage, q, i)
                w = kview(big[stage][0])
                view = raw[:, slot, :].rearrange("p (o k n) -> p o k n", o=1, k=KD)
                for part in range(2):
                    sp.dma_start(view[:, :, :, part * UPW:(part + 1) * UPW],
                                 w[:, ds(l, 1), :, ds(part * FF + UPW * (q + 2 * i), UPW)]
                                 ).then_inc(raw_arrived[slot].sem, 16)
                if not isinstance(i, int) or q + 2 * i < ADA_STEPS:
                    load_ada(l, stage, q, i)

            def load_rows(l, stage):
                sp.wait_ge(ht_lo.sem, ht_lo.at(l, 4 * stage + 4))
                g = norm_g.rearrange("l s n -> (l s) n")[ds(l * 6 + 2 * stage + 1, 1), :]
                b = ada_b.rearrange("l (m n) -> (l m) n", n=D)[ds(l * 9 + 3 * stage + 2, 1), :]
                sp.dma_start(gain[:], g.to_broadcast([128, D])).then_inc(rows_arrived.sem, 16)
                sp.dma_start(tmp[:, 0, :], b.to_broadcast([128, D])).then_inc(rows_arrived.sem, 16)

            def ffn(l, stage):
                for q in range(2):
                    load_up(l, stage, q)
                for q in range(2, 4):
                    load_up(l, stage, q)
                load_rows(l, stage)
                with sp.Fori(0, (N_UP - 5) // 2) as i:
                    for q in (4, 5):
                        load_up(l, stage, q, i)
                load_up(l, stage, N_UP - 1)
                for q in range(N_UP, FFN_STEPS):
                    slot = wait_raw_slot(l, stage, q, 0)
                    blocks = down_blocks(q)
                    half = len(blocks) // 2
                    cut = half
                    for b in range(1, len(blocks)):
                        if blocks[b][0] != blocks[b - 1][0]:
                            cut = b
                    w = kview(big[stage][1])
                    for b0, b1 in ((0, cut), (cut, len(blocks))):
                        n, k = blocks[b0]
                        load_blocks(slot, b0 * 512, w, l, k, k + b1 - b0, n * 512, 512)
                    if q < ADA_STEPS:
                        load_ada(l, stage, q, 0)

            def mix(l):
                win = kview(w_in)
                for q in range(MIX_STEPS):
                    slot = wait_raw_slot(l, 1, q, 0)
                    if q == UQ:
                        w = w_uq.rearrange("l k n -> k l n")
                        w2 = w_uq[:, 0:256, :].rearrange("l (k p) n -> p l k n", p=128)
                        load_blocks(slot, 0, w2, l, 0, 2, 0, H * QKD)
                        dst = raw[0:QL - 256, slot, 1536:2304].rearrange("p (o n) -> p o n", o=1)
                        sp.dma_start(dst, w[256:QL, ds(l, 1), :]).then_inc(raw_arrived[slot].sem, 16)
                    elif q == UKV:
                        for n in range(2):
                            load_blocks(slot, 512 * n, kview(w_ukv), l, 0, 1, 512 * n, 512)
                    elif q >= 18:
                        for k in (0, 4):
                            load_blocks(slot, 512 * k, kview(w_out), l, k, k + 4, 512 * (q - 18), 512)
                    elif q < 4:
                        for k in (0, 4):
                            load_blocks(slot, 512 * k, win, l, k, k + 4, 512 * q, 512)
                    else:
                        br, part = next((b, q - s) for b, s in BRANCH_STEPS.items() if 0 <= q - s < 3)
                        if part < 2:
                            for k in (0, 4):
                                load_blocks(slot, 512 * k, win, l, k, k + 4, MIX + br * D + 512 * part, 512)
                        else:
                            w = kview((w_a, w_b, w_c, w_d)[br])
                            step = w.shape[2] // 2
                            for k in range(2):
                                load_blocks(slot, k * step * D, w, l, k * step, (k + 1) * step, 0, D)
                    if q in MIX_ADA:
                        load_ada(l, 1, MIX_ADA.index(q), 0)
                    if q == 1:
                        load_rows(l, 1)
                        sp.dma_start(poolw[:].rearrange("p (o g) n -> p o g n", o=1),
                                     pool_w.rearrange("l g c d -> c l g d")[:, ds(l, 1), :, :]
                                     ).then_inc(poolw_arrived.sem, 16)

            with sp.Fori(0, L) as l:
                ffn(l, 0)
                mix(l)
                ffn(l, 2)
            sp.wait_ge(x_updated.sem, x_updated.at(L, 0))
            for t in range(2):
                sp.dma_start(out[0, t * 128:(t + 1) * 128, :], xs[:, t, :]).then_inc(out_stored, 16)
            sp.wait_ge(out_stored, 32)

        @block.scalar
        def _(act):
            copy = lambda o, i: nc.scalar.activation(o, i, ACT.Copy)

            act.dma_start(xs[:, :, :], x[0].rearrange("(t p) n -> p t n", p=128)).then_inc(x_arrived, 16)
            act.wait_ge(rows_clear, 1)
            n_rows = 0
            for l in range(L):
                parts = [(V_G + 8 * s, norm_g[l, 2 * s, :].rearrange("(k p) -> k p", p=128)) for s in range(3)]
                parts += [(V_B, ada_b[l, :].rearrange("(k p) -> k p", p=128)),
                          (V_CB, conv_b[l, :].rearrange("(k p) -> k p", p=128)),
                          (V_LG, conv_ln_g[l, :].rearrange("(k p) -> k p", p=128)),
                          (V_LB, conv_ln_b[l, :].rearrange("(k p) -> k p", p=128)),
                          (V_PS, pool_scale[l, :].rearrange("(k p) -> k p", p=128)),
                          (V_QG, q_norm_g[l, 0:256].rearrange("(k p) -> k p", p=128)),
                          (V_KG, kv_norm_g[l, :].rearrange("(k p) -> k p", p=128))]
                for r, src in parts:
                    act.dma_start(rows[r:r + src.shape[0], l, :], src).then_inc(vrows_arrived, 16)
                    n_rows += 1
                act.dma_start(rows[V_QG + 2:V_QG + 3, l, 0:QL - 256],
                              q_norm_g[l:l + 1, 256:QL]).then_inc(vrows_arrived, 16)
                act.dma_start(crows[:, l, :], conv_w[l].rearrange("t (k p) -> (t k) p", p=128)
                              ).then_inc(vrows_arrived, 16)
                n_rows += 2
            assert n_rows == 24
            act.dma_start(ident[:], ident_c).then_inc(consts_arrived, 16)
            act.dma_start(dft[:, :, :], dft_c.rearrange("(k p) n -> p k n", p=128)).then_inc(consts_arrived, 16)
            act.dma_start(chan[:, :, :], chan_c.rearrange("p (k n) -> p k n", k=2)).then_inc(consts_arrived, 16)
            act.dma_start(band[:, :, :, :], band_c).then_inc(consts_arrived, 16)
            act.dma_start(rope[:, :, :, :], rope_c.rearrange("(t p) a b -> p t a b", p=128)
                          ).then_inc(consts_arrived, 16)
            act.wait_ge(c_arrived, 16)
            nc.scalar.activation(c_act[:], c_raw[:], ACT.Silu).then_inc(c_ready, 1)

            def split(l, stage, q, i=0, quarters=range(4)):
                panel, slot, visit = stage_panel(stage, q, i)
                act.wait_ge(raw_arrived[slot].sem, raw_arrived[slot].at(l, 32 * (visit + 1)))
                before = MM_BEFORE[STAGE_PANEL[stage] + q - 1] if STAGE_PANEL[stage] + q >= 1 \
                    else -2 * segments(-1)
                act.wait_ge(mm_done.sem, mm_done.at(l, before + 4 * i))
                for n in quarters:
                    parts, a, b = pieces(stage, q)[n]
                    copy(w_hi[0:parts, slot, a:b], raw[0:parts, slot, a:b]).then_inc(hi_done.sem, 1)

            def enter(l, stage):
                for t in range(2):
                    act.wait_ge(x_updated.sem, x_updated.at(l, 2 * stage + t - 1))
                    if t:
                        act.wait_ge(ssx_ready.sem, ssx_ready.at(l, 2 * stage + t))
                    nc.scalar.activation(junk[:], xs[:, t, :], ACT.Square,
                                         accum_out=ssx[:, t:t + 1]).then_inc(ssx_ready.sem, 1)
                if stage == 0:
                    split(l, 0, 0, quarters=(2, 3))
                act.wait_ge(ab_ready.sem, ab_ready.at(l, stage + 1))
                for t in range(2):
                    act.wait_ge(ht_filled.sem, ht_filled.at(l, 4 * stage + 2 * t + 2))
                    for k in range(4):
                        ins = nc.scalar.activation(tmp[:, t, k * 128:(k + 1) * 128],
                                                   T[2 * t][:, k * 128:(k + 1) * 128], ACT.Identity,
                                                   scale=ab[:, 2, k:k + 1], bias=ab[:, 0, k:k + 1])
                    ins.then_inc(hf_act.sem, 1)
                    for half in range(2):
                        own, other = (hf_act, hf_dve)
                        w = own if half == 0 else other
                        act.wait_ge(w.sem, w.at(l, 2 * stage + t + 1))
                        copy(hT_hi[:, 4 * half:4 * half + 4, t * 128:(t + 1) * 128],
                             tmp[:, t, half * 512:(half + 1) * 512].rearrange("p (k n) -> p k n", k=4)
                             ).then_inc(ht_hi.sem, 1)

            def leave(l, stage, q0, q1, n):
                seg = 0
                for t in range(2):
                    act.wait_ge(mm_done.sem, mm_done.at(l, mm_group(stage, q0, q1, t)))
                    g = (N_UP if stage != 1 else 24) + n
                    if n or t:
                        act.wait_ge(ssy_ready.sem, ssy_ready.at(l, 4 * stage + 2 * n + t))
                    nc.scalar.activation(junk[:, 0:512], Z[pair_of(stage, g)][t][:], ACT.Square,
                                         accum_out=ssy[:, t, n:n + 1]).then_inc(ssy_ready.sem, 1)

            def silu(l, stage, q, i=0):
                par = pair_of(stage, q)
                hp = q % 2
                if q >= 4:
                    act.wait_ge(hid_filled.sem, hid_filled.at(l, N_UP * (stage // 2) + q - 3 + 2 * i))
                for t in range(2):
                    act.wait_ge(mm_done.sem, mm_done.at(l, mm_group(stage, q - 2, 0, t) + 4 * i))
                    nc.scalar.activation(hid[:, hp, t, :], Z[par][t][:, 0:UPW], ACT.Silu
                                         ).then_inc(silu_ready.sem, 1)

            def hidden_hi(l, stage, q, i=0):
                act.wait_ge(hid_filled.sem, hid_filled.at(l, N_UP * (stage // 2) + q - 2 + 2 * i))
                chunk = hid_hi[:, :, :].rearrange("p k n -> p (k n)")[:, ds((q - 3 + 2 * i) * 512, 512)]
                copy(chunk, T[(q - 3) % 2][:]).then_inc(hid_hi_ready.sem, 1)

            def ffn(l, stage):
                enter_split(l, stage)
                for q in range(2, 4):
                    split(l, stage, q)
                    silu(l, stage, q)
                    if q >= 3:
                        hidden_hi(l, stage, q)
                with act.Fori(0, (N_UP - 5) // 2) as i:
                    for q in (4, 5):
                        split(l, stage, q, i)
                        silu(l, stage, q, i)
                        hidden_hi(l, stage, q, i)
                for q in range(N_UP - 1, FFN_STEPS):
                    split(l, stage, q)
                    if q - 2 < N_UP:
                        silu(l, stage, q)
                    if q - 3 < N_UP:
                        hidden_hi(l, stage, q)
                    if q == FFN_GROUPS_SPLIT + 2:
                        leave(l, stage, FFN_GROUPS_SPLIT, 0, 0)
                next_first(l, stage)
                leave(l, stage, FFN_STEPS - 1, 0, 1)

            def next_first(l, stage):
                if stage < 2:
                    split(l, stage + 1, 0)

            def enter_split(l, stage):
                if stage == 0:
                    split(l, 0, 0, quarters=(0, 1))
                enter(l, stage)
                split(l, stage, 1)

            def mix(l):
                enter_split(l, 1)
                mmw = lambda q, seg, t: act.wait_ge(mm_done.sem, mm_done.at(l, mm_group(1, q, seg, t)))

                def gate(q, n):
                    br = next(b for b, s in BRANCH_STEPS.items() if 0 <= q - s < 3)
                    g = 8 + 4 * (3 - br) + n
                    for t in range(2):
                        mmw(q, 0, t)
                        if br < 3:
                            act.wait_ge(merged_done.sem, merged_done.at(l, 4 * (2 - br) + 2 * n + t + 1))
                        nc.scalar.activation(gates[:, t, n * 512:(n + 1) * 512], Z[pair_of(1, g)][t][:],
                                             ACT.Sigmoid).then_inc(gate_ready.sem, 1)

                def q_copy(n):
                    for t in range(2):
                        mmw(UQ, n, t)
                        w = (512, 256)[n]
                        copy(qf[:, t, 512 * n:512 * n + w], Z[pair_of(1, 4 + n)][t][:, 0:w]
                             ).then_inc(q_copied.sem, 1)

                def kv_copy(n):
                    for t in range(2):
                        mmw(UKV, n, t)
                        kv = Z[pair_of(1, 6 + n)][t][:].rearrange("p (h d) -> p h d", h=4)
                        copy(kf[:, t, :].rearrange("p (h d) -> p h d", h=H)[:, 4 * n:4 * n + 4, 0:NOPE],
                             kv[:, :, 0:NOPE])
                        copy(v[:, t, :].rearrange("p (h d) -> p h d", h=H)[:, 4 * n:4 * n + 4, :],
                             kv[:, :, NOPE:NOPE + VH]).then_inc(kv_copied.sem, 1)

                def exps(i):
                    act.wait_ge(nmx_ready.sem, nmx_ready.at(l, i + 1))
                    if i >= 1:
                        act.wait_ge(pT_filled.sem, pT_filled.at(l, 2 * i))
                    for h in range(4):
                        ins = nc.scalar.activation(p[:, h, :], T[2 + h // 2][:, (h % 2) * 256:(h % 2) * 256 + 256],
                                                   ACT.Exp, bias=nmx[:, h:h + 1], scale=QKD ** -0.5,
                                                   accum_out=rs[:, h:h + 1])
                    ins.then_inc(exp_done.sem, 1)

                def pT_copy(i):
                    act.wait_ge(pT_filled.sem, pT_filled.at(l, 2 * i + 1))
                    copy(pT[:, 0, :, :], T[0][:].rearrange("p (h n) -> p h n", h=4)).then_inc(pT_act.sem, 1)

                def o_copy(i):
                    act.wait_ge(o_done.sem, o_done.at(l, i + 1))
                    t, hh = i // 2, i % 2
                    copy(oT_hi[:, 2 * hh:2 * hh + 2, t * 128:(t + 1) * 128],
                         T[0][:, 0:256].rearrange("p (c n) -> p c n", c=2)).then_inc(o_hi.sem, 1)

                def kq_copy(f):
                    act.wait_ge(kq_filled.sem, kq_filled.at(l, f + 1))
                    dst = kT if f < 4 else qT
                    t, hh = (f % 4) // 2, f % 2
                    bank = T[(2, 3, 0, 1)[f % 4]]
                    copy(dst[0:QKD, 4 * hh:4 * hh + 4, t * 128:(t + 1) * 128],
                         bank[0:QKD, :].rearrange("p (h n) -> p h n", h=4)).then_inc(kq_act.sem, 1)

                for q in range(2, MIX_STEPS):
                    if q not in (2, 3, 4):
                        split(l, 1, q)
                    if q == 2:
                        for t in range(2):
                            mmw(0, 0, t)
                            za_bank = Z[pair_of(1, 0)][t]
                            copy(za[:, t, :], za_bank[:]).then_inc(za_copied.sem, 1)
                            nc.scalar.activation(junk[:, 512 * t:512 * t + QL], za_bank[:, 0:QL], ACT.Square,
                                                 accum_out=ssa[:, t, 0:1])
                            nc.scalar.activation(junk[:, 512 * t + QL:512 * t + 512 - ROPE], za_bank[:, QL:QL + KVL], ACT.Square,
                                                 accum_out=ssa[:, t, 1:2]).then_inc(ssa_ready.sem, 1)
                        split(l, 1, q)
                    if q == 3:
                        for t in range(2):
                            mmw(1, 0, t)
                            nc.scalar.activation(u[:, t, :], Z[pair_of(1, 1)][t][:, CC:2 * CC], ACT.Sigmoid
                                                 ).then_inc(sgb_ready.sem, 1)
                        split(l, 1, q)
                    if q == 4:
                        act.wait_ge(an_filled.sem, an_filled.at(l, 2))
                        for k in range(4):
                            r = QL - 256 if k == 2 else 128
                            nc.scalar.activation(aT_hi[0:r, k, :], T[k // 2][0:r, (k % 2) * 256:(k % 2) * 256 + 256],
                                                 ACT.Copy, scale=vec[0:r, V_QG + k:V_QG + k + 1]
                                                 ).then_inc(a_hi.sem, 1)
                        split(l, 1, q)
                        for t in range(2):
                            mmw(2, 0, t)
                            copy(zt[:, t, 0, :], Z[pair_of(1, 2)][t][:]).then_inc(zt_copied.sem, 1)
                        act.wait_ge(u_filled.sem, u_filled.at(l, 1))
                        copy(uT[:, :, CW // 2:CW // 2 + S], T[2][:].rearrange("p (c n) -> p c n", c=2)
                             ).then_inc(uT_ready.sem, 1)
                    if q == 5:
                        for t in range(2):
                            mmw(3, 0, t)
                            copy(zt[:, t, 1, :], Z[pair_of(1, 3)][t][:]).then_inc(zt_copied.sem, 1)
                        act.wait_ge(pool1_done.sem, pool1_done.at(l, 1))
                        copy(dT[:, 0:2, :], T[0][:].rearrange("p (g n) -> p g n", g=2)).then_inc(dT_act.sem, 1)
                        q_copy(0)
                    if q == 6:
                        q_copy(1)
                        for g in (0, 2):
                            act.wait_ge(fnet1_done.sem, fnet1_done.at(l, g + 1))
                            copy(U[:, g, :], T[(2, 3, 0, 1)[g]][:]).then_inc(U_act.sem, 1)
                        kv_copy(0)
                    if q == 7:
                        kv_copy(1)
                    if q in (8, 9, 11, 12, 14, 15, 17, 18):
                        gate(q - 2, (q - 2) % 3)
                    if q == 8:
                        act.wait_ge(fnet2_done.sem, fnet2_done.at(l, 2))
                        for b in range(2):
                            copy(bT_hi[:, 2 * b:2 * b + 2, :], T[b][:].rearrange("p (g n) -> p g n", g=2)
                                 ).then_inc(b_hi.sem, 1)
                        kq_copy(0)
                    if q == 9:
                        kq_copy(2)
                        kq_copy(4)
                    if q == 10:
                        kq_copy(6)
                        exps(0)
                    if q == 11:
                        act.wait_ge(pool2_done.sem, pool2_done.at(l, 2))
                        act.wait_ge(mm_done.sem, mm_done.at(l, mm_group(1, 8, 1, 1)))
                        for g in range(4):
                            ins = nc.scalar.activation(bT_hi[:, g, :], T[2 + g // 2][:, (g % 2) * 256:(g % 2) * 256 + 256],
                                                       ACT.Copy, scale=vec[:, V_PS + g:V_PS + g + 1])
                            if g % 2:
                                ins.then_inc(b_hi.sem, 1)
                        pT_copy(0)
                    if q == 12:
                        o_copy(0)
                        exps(1)
                    if q == 13:
                        pT_copy(1)
                    if q == 14:
                        o_copy(1)
                        act.wait_ge(lnx_filled.sem, lnx_filled.at(l, 1))
                        for k in range(2):
                            ins = nc.scalar.activation(sgv[:, k, :], T[1][:, k * 256:(k + 1) * 256], ACT.Sigmoid,
                                                       scale=vec[:, V_LG + k:V_LG + k + 1],
                                                       bias=vec[:, V_LB + k:V_LB + k + 1])
                        ins.then_inc(sgv_ready.sem, 1)
                        act.wait_ge(lnv_ready.sem, lnv_ready.at(l, 1))
                        act.wait_ge(mm_done.sem, mm_done.at(l, mm_group(1, 11, 1, 1)))
                        copy(bT_hi[:, 0:2, :], lnv[:, :, :]).then_inc(b_hi.sem, 1)
                        exps(2)
                    if q == 15:
                        pT_copy(2)
                    if q == 16:
                        o_copy(2)
                        exps(3)
                    if q == 17:
                        pT_copy(3)
                        o_copy(3)
                    if q == 18:
                        for f in range(4):
                            act.wait_ge(m_filled.sem, m_filled.at(l, f + 1))
                            kh, t = f // 2, f % 2
                            copy(hT_hi[:, 4 * kh:4 * kh + 4, t * 128:(t + 1) * 128],
                                 T[f][:].rearrange("p (k n) -> p k n", k=4)).then_inc(m_hi.sem, 1)
                leave(l, 1, 18, 0, 0)
                next_first(l, 1)
                leave(l, 1, 19, 0, 1)

            act.wait_ge(x_arrived, 16)
            with act.Fori(0, L) as l:
                ffn(l, 0)
                mix(l)
                ffn(l, 2)

        @block.vector
        def _(dve):
            tt = nc.vector.tensor_tensor
            stt = nc.vector.scalar_tensor_tensor
            tsc = nc.vector.tensor_scalar
            chain = dve_chain
            chain.per_layer = DVE_CHAIN_LAYER

            def split(l, stage, q, i=0, quarters=range(4)):
                panel, slot, _ = stage_panel(stage, q, i)
                for n in quarters:
                    parts, a, b = pieces(stage, q)[n]
                    dve.wait_ge(hi_done.sem, hi_done.at(l, 4 * panel + n + 1))
                    tt(w_lo[0:parts, slot, a:b], raw[0:parts, slot, a:b],
                       w_hi[0:parts, slot, a:b].bitcast(f32), ALU.subtract).then_inc(lo_done.sem, 1)

            def ada_step(l, stage, q, i=0, loop_links=0):
                half = q // 2 + i
                if stage == 1 and q >= 8:
                    half = q // 2 - 4
                acc = modacc[:].rearrange("p h n -> p (h n)")[:, ds(half * 512, 512)]
                for e in range(2):
                    dve.wait_ge(ada_arrived[e].sem,
                                ada_arrived[e].at(l, 16 * (ADA_STEPS * stage + q + 2 * i + 1)))
                    for r in range(2):
                        j = 4 * (q % 2) + 2 * e + r
                        if j == 0:
                            ins = tsc(acc, ada[:, e, r, :], c_act[:, 0:1], None, ALU.mult)
                        else:
                            ins = stt(acc, ada[:, e, r, :], c_act[:, j:j + 1], acc, ALU.mult, ALU.add)
                        if r == 0:
                            chain.link(ins)
                        else:
                            ins.then_inc(ada_done.sem, 1)
                            dve.wait_ge(ada_done.sem,
                                        ada_done.at(l, 2 * (ADA_STEPS * stage + q + 2 * i) + e + 1))

            def enter(l, stage):
                shift, scale = V_B + 24 * stage, V_B + 24 * stage + 8
                dve.wait_ge(mods_read.sem, mods_read.at(l, stage))
                tt(ab[:, 0, :], mods[:, 0:8], vec[:, shift:shift + 8], ALU.add)
                chain.link(tt(ab[:, 1, :], mods[:, 8:16], vec[:, scale:scale + 8], ALU.add))
                stt(ab[:, 2, :], ab[:, 1, :], 1.0, vec[:, V_G + 8 * stage:V_G + 8 * stage + 8],
                    ALU.add, ALU.mult).then_inc(ab_ready.sem, 1)
                for t in range(2):
                    dve.wait_ge(rsx_ready.sem, rsx_ready.at(l, 2 * stage + t + 1))
                    tsc(tmp[:, t, :], xs[:, t, :], rsx[:, t:t + 1], None, ALU.mult
                        ).then_inc(xn_ready.sem, 1)
                if stage == 0:
                    split(l, 0, 0, quarters=(2, 3))
                dve.wait_ge(ab_ready.sem, ab_ready.at(l, stage + 1))
                for t in range(2):
                    dve.wait_ge(ht_filled.sem, ht_filled.at(l, 4 * stage + 2 * t + 2))
                    for k in range(4, 8):
                        ins = tsc(tmp[:, t, k * 128:(k + 1) * 128],
                                  T[2 * t + 1][:, (k - 4) * 128:(k - 3) * 128],
                                  ab[:, 2, k:k + 1], ab[:, 0, k:k + 1], ALU.mult, ALU.add)
                    ins.then_inc(hf_dve.sem, 1)
                    for half in range(2):
                        dve.wait_ge(ht_hi.sem, ht_hi.at(l, 4 * stage + 2 * t + half + 1))
                        sl = (slice(None), slice(4 * half, 4 * half + 4), slice(t * 128, (t + 1) * 128))
                        tt(hT_lo[sl], tmp[:, t, half * 512:(half + 1) * 512].rearrange("p (k n) -> p k n", k=4),
                           hT_hi[sl].bitcast(f32), ALU.subtract).then_inc(ht_lo.sem, 1)

            def scaled_y(l, stage, q0, q1, n):
                for t in range(2):
                    dve.wait_ge(ssy_ready.sem, ssy_ready.at(l, 4 * stage + 2 * n + t + 1))
                    g = (N_UP if stage != 1 else 24) + n
                    tt(tmp[:, t, n * 512:(n + 1) * 512], Z[pair_of(stage, g)][t][:],
                       gain[:, n * 512:(n + 1) * 512], ALU.mult).then_inc(y_scaled.sem, 1)

            def update_x(l, stage):
                dve.wait_ge(y_scaled.sem, y_scaled.at(l, 4 * stage + 4))
                for t in range(2):
                    dve.wait_ge(rsy_ready.sem, rsy_ready.at(l, 2 * stage + t + 1))
                    stt(xs[:, t, :], tmp[:, t, :], rsy[:, t:t + 1], xs[:, t, :], ALU.mult, ALU.add
                        ).then_inc(x_updated.sem, 1)

            def make_gain(l, stage):
                dve.wait_ge(rows_arrived.sem, rows_arrived.at(l, 32 * stage + 32))
                for n in range(2):
                    dve.wait_ge(gain_summed.sem, gain_summed.at(l, 2 * stage + n + 1))
                    sl = slice(n * 512, (n + 1) * 512)
                    bank = (T[2], T[3]) if stage != 1 else (T[0], T[1])
                    tt(tmp[:, 0, sl], bank[n][:], tmp[:, 0, sl], ALU.add).then_inc(gain_read.sem, 1)
                dve.wait_ge(gain_read.sem, gain_read.at(l, 2 * stage + 2))
                chain.link(stt(gain[:], tmp[:, 0, :], 1.0 if stage == 1 else 0.5, gain[:], ALU.mult, ALU.mult))

            def read_mods(l, stage):
                dve.wait_ge(cols_summed.sem, cols_summed.at(l, stage + 1))
                nc.vector.tensor_copy(mods[:], T[0 if stage == 1 else 2][:, 0:16]).then_inc(mods_read.sem, 1)

            def gated_hidden(l, stage, q, i=0):
                base = 2 * N_UP * (stage // 2) + 2 * (q - 2) + 4 * i
                for t in range(2):
                    dve.wait_ge(silu_ready.sem, silu_ready.at(l, base + t + 1))
                    tt(hid[:, q % 2, t, :], hid[:, q % 2, t, :], Z[pair_of(stage, q)][t][:, UPW:2 * UPW],
                       ALU.mult).then_inc(hid_ready.sem, 1)

            def hidden_lo(l, stage, q, i=0):
                dve.wait_ge(hid_hi_ready.sem, hid_hi_ready.at(l, N_UP * (stage // 2) + q - 2 + 2 * i))
                at_ = (q - 3 + 2 * i) * 512
                tt(hid_lo[:, :, :].rearrange("p k n -> p (k n)")[:, ds(at_, 512)], T[(q - 3) % 2][:],
                   hid_hi[:, :, :].rearrange("p k n -> p (k n)")[:, ds(at_, 512)].bitcast(f32),
                   ALU.subtract).then_inc(hid_lo_ready.sem, 1)

            def ffn(l, stage):
                if stage == 0:
                    split(l, 0, 0, quarters=(0, 1))
                enter(l, stage)
                split(l, stage, 1)
                ada_step(l, stage, 0)
                ada_step(l, stage, 1)
                for q in range(2, 4):
                    split(l, stage, q)
                    gated_hidden(l, stage, q)
                    if q >= 3:
                        hidden_lo(l, stage, q)
                    ada_step(l, stage, q)
                before = chain.n
                pass_waits(dve, "dve")
                with dve.Fori(0, (N_UP - 5) // 2) as i:
                    chain.extra = i * LOOP_LINKS
                    for q in (4, 5):
                        split(l, stage, q, i)
                        gated_hidden(l, stage, q, i)
                        hidden_lo(l, stage, q, i)
                        ada_step(l, stage, q, i)
                    assert chain.n - before == LOOP_LINKS, chain.n - before
                chain.extra = 0
                chain.n = before + LOOP_LINKS * ((N_UP - 5) // 2)
                for q in range(N_UP - 1, FFN_STEPS):
                    split(l, stage, q)
                    if q - 2 < N_UP:
                        gated_hidden(l, stage, q)
                    if q - 3 < N_UP:
                        hidden_lo(l, stage, q)
                    if q < ADA_STEPS:
                        ada_step(l, stage, q)
                    if q == FFN_GROUPS_SPLIT:
                        make_gain(l, stage)
                    if q == FFN_GROUPS_SPLIT + 2:
                        read_mods(l, stage)
                        scaled_y(l, stage, FFN_GROUPS_SPLIT, 0, 0)
                if stage < 2:
                    split(l, stage + 1, 0)
                scaled_y(l, stage, FFN_STEPS - 1, 0, 1)
                update_x(l, stage)

            def mix(l):
                enter(l, 1)
                split(l, 1, 1)
                ada_step(l, 1, 0)
                ada_step(l, 1, 1)

                def merge(q, n):
                    br = next(b for b, s in BRANCH_STEPS.items() if 0 <= q - s < 3)
                    g = 8 + 4 * (3 - br) + 2 + n
                    for t in range(2):
                        dve.wait_ge(gate_ready.sem, gate_ready.at(l, 4 * (3 - br) + 2 * n + t + 1))
                        dve.wait_ge(mm_done.sem, mm_done.at(l, mm_group(1, q, n, t)))
                        sl = slice(n * 512, (n + 1) * 512)
                        if br == 3:
                            tt(tmp[:, t, sl], gates[:, t, sl], Z[pair_of(1, g)][t][:], ALU.mult
                               ).then_inc(merged_done.sem, 1)
                        else:
                            chain.link(tt(gates[:, t, sl], gates[:, t, sl], Z[pair_of(1, g)][t][:], ALU.mult))
                            tt(tmp[:, t, sl], tmp[:, t, sl], gates[:, t, sl], ALU.add
                               ).then_inc(merged_done.sem, 1)

                def conv_taps(first, last):
                    for tap in range(first, last):
                        for k in range(2):
                            w = vec[:, V_CW + 2 * tap + k:V_CW + 2 * tap + k + 1]
                            src = uT[:, k, tap:tap + S]
                            if tap == 0:
                                ins = tsc(yc[:, k, :], src, w, vec[:, V_CB + k:V_CB + k + 1], ALU.mult, ALU.add)
                            else:
                                ins = stt(yc[:, k, :], src, w, yc[:, k, :], ALU.mult, ALU.add)
                        if tap == CW - 1:
                            ins.then_inc(yc_ready.sem, 1)
                        else:
                            chain.link(ins)

                def row_max(i):
                    for b in range(2):
                        dve.wait_ge(scores_done.sem, scores_done.at(l, 2 * i + b + 1))
                        ins = nc.vector.reduce_max(mx[:, 2 * b:2 * b + 2],
                                                   T[2 + b][:].rearrange("p (h n) -> p h n", h=2), axis=AX.X)
                    chain.link(ins)
                    tsc(nmx[:], mx[:], -(QKD ** -0.5), None, ALU.mult).then_inc(nmx_ready.sem, 1)

                def normalise(i):
                    dve.wait_ge(exp_done.sem, exp_done.at(l, i + 1))
                    chain.link(nc.vector.reciprocal(rinv[:], rs[:]))
                    tt(p[:, :, :], p[:, :, :], rinv[:].unsqueeze(2).to_broadcast([128, 4, S]), ALU.mult
                       ).then_inc(p_ready.sem, 1)

                def pT_copy(i):
                    dve.wait_ge(pT_filled.sem, pT_filled.at(l, 2 * i + 2))
                    nc.vector.tensor_copy(pT[:, 1, :, :], T[1][:].rearrange("p (h n) -> p h n", h=4)
                                          ).then_inc(pT_dve.sem, 1)

                def o_rest(i):
                    t, hh = i // 2, i % 2
                    dve.wait_ge(o_hi.sem, o_hi.at(l, i + 1))
                    sl = (slice(None), slice(2 * hh, 2 * hh + 2), slice(t * 128, (t + 1) * 128))
                    tt(oT_lo[sl], T[0][:, 0:256].rearrange("p (c n) -> p c n", c=2), oT_hi[sl].bitcast(f32),
                       ALU.subtract).then_inc(o_lo.sem, 1)

                def kq_copy(f):
                    dve.wait_ge(kq_filled.sem, kq_filled.at(l, f + 1))
                    dst = kT if f < 4 else qT
                    t, hh = (f % 4) // 2, f % 2
                    bank = T[(2, 3, 0, 1)[f % 4]]
                    nc.vector.tensor_copy(dst[0:QKD, 4 * hh:4 * hh + 4, t * 128:(t + 1) * 128],
                                          bank[0:QKD, :].rearrange("p (h n) -> p h n", h=4)
                                          ).then_inc(kq_dve.sem, 1)

                for q in range(2, MIX_STEPS):
                    if q not in (3, 4):
                        split(l, 1, q)
                    if q == 2:
                        for t in range(2):
                            dve.wait_ge(rsa_ready.sem, rsa_ready.at(l, t + 1))
                            tsc(za[:, t, 0:QL], za[:, t, 0:QL], rsa[:, t, 0:1], None, ALU.mult)
                            tsc(za[:, t, QL:QL + KVL], za[:, t, QL:QL + KVL], rsa[:, t, 1:2], None, ALU.mult
                                ).then_inc(an_ready.sem, 1)
                        for side in (slice(0, CW // 2), slice(CW // 2 + S, PADW)):
                            ins = nc.vector.memset(uT[:, :, side], 0.0)
                        chain.link(ins)
                    if q == 3:
                        for t in range(2):
                            dve.wait_ge(sgb_ready.sem, sgb_ready.at(l, t + 1))
                            tt(u[:, t, :], u[:, t, :], Z[pair_of(1, 1)][t][:, 0:CC], ALU.mult
                               ).then_inc(u_ready.sem, 1)
                        split(l, 1, q)
                    if q == 4:
                        for k in range(4):
                            r = QL - 256 if k == 2 else 128
                            dve.wait_ge(a_hi.sem, a_hi.at(l, 2 * (k // 2) + 2))
                            stt(aT_lo[0:r, k, :], T[k // 2][0:r, (k % 2) * 256:(k % 2) * 256 + 256],
                                vec[0:r, V_QG + k:V_QG + k + 1], aT_hi[0:r, k, :].bitcast(f32),
                                ALU.mult, ALU.subtract).then_inc(a_lo.sem, 1)
                        split(l, 1, q)
                        dve.wait_ge(uT_ready.sem, uT_ready.at(l, 1))
                        conv_taps(0, 4)
                    if q == 5:
                        dve.wait_ge(pool1_done.sem, pool1_done.at(l, 2))
                        nc.vector.tensor_copy(dT[:, 2:4, :], T[1][:].rearrange("p (g n) -> p g n", g=2)
                                              ).then_inc(dT_dve.sem, 1)
                        conv_taps(4, 9)
                    if q == 6:
                        for g in (1, 3):
                            dve.wait_ge(fnet1_done.sem, fnet1_done.at(l, g + 1))
                            nc.vector.tensor_copy(U[:, g, :], T[(2, 3, 0, 1)[g]][:]).then_inc(U_dve.sem, 1)
                        conv_taps(9, 14)
                    if q == 7:
                        make_gain(l, 1)
                        conv_taps(14, 20)
                    if q == 8:
                        dve.wait_ge(k_rotated.sem, k_rotated.at(l, 2))
                        for b in range(2):
                            dve.wait_ge(b_hi.sem, b_hi.at(l, b + 1))
                            tt(bT_lo[:, 2 * b:2 * b + 2, :], T[b][:].rearrange("p (g n) -> p g n", g=2),
                               bT_hi[:, 2 * b:2 * b + 2, :].bitcast(f32), ALU.subtract).then_inc(b_lo.sem, 1)
                        kq_copy(1)
                        conv_taps(20, 24)
                    if q == 9:
                        kq_copy(3)
                        kq_copy(5)
                        conv_taps(24, 27)
                        merge(8, 0)
                    if q == 10:
                        kq_copy(7)
                        row_max(0)
                        merge(8, 1)
                        normalise(0)
                        conv_taps(27, 31)
                    if q == 11:
                        for b in range(2):
                            dve.wait_ge(b_hi.sem, b_hi.at(l, 3 + b))
                            for g in (2 * b, 2 * b + 1):
                                ins = stt(bT_lo[:, g, :], T[2 + b][:, (g % 2) * 256:(g % 2) * 256 + 256],
                                          vec[:, V_PS + g:V_PS + g + 1], bT_hi[:, g, :].bitcast(f32),
                                          ALU.mult, ALU.subtract)
                            ins.then_inc(b_lo.sem, 1)
                        pT_copy(0)
                    if q == 12:
                        o_rest(0)
                        row_max(1)
                        dve.wait_ge(yc_filled.sem, yc_filled.at(l, 1))
                        for t in range(2):
                            ins = nc.vector.bn_stats(bns[:, t, :], T[1][:, t * 256:(t + 1) * 256])
                        chain.link(ins)
                        pass_waits(dve, "dve")
                        for t in range(2):
                            ins = nc.vector.bn_aggr(mv[:, t, :], bns[:, t, :])
                        ins.then_inc(mv_ready.sem, 1)
                        normalise(1)
                        dve.wait_ge(rsc_ready.sem, rsc_ready.at(l, 1))
                        for t in range(2):
                            ins = tsc(lnx[:, t, :], T[1][:, t * 256:(t + 1) * 256], mv[:, t, 0:1], rsc[:, t:t + 1],
                                      ALU.subtract, ALU.mult)
                        ins.then_inc(lnx_ready.sem, 1)
                        merge(11, 0)
                    if q == 13:
                        pT_copy(1)
                        merge(11, 1)
                    if q == 14:
                        o_rest(1)
                        dve.wait_ge(sgv_ready.sem, sgv_ready.at(l, 1))
                        for k in range(2):
                            ins = tsc(lnv[:, k, :], T[1][:, k * 256:(k + 1) * 256], vec[:, V_LG + k:V_LG + k + 1],
                                      vec[:, V_LB + k:V_LB + k + 1], ALU.mult, ALU.add)
                        chain.link(ins)
                        tt(lnv[:, :, :], lnv[:, :, :], sgv[:, :, :], ALU.mult).then_inc(lnv_ready.sem, 1)
                        dve.wait_ge(b_hi.sem, b_hi.at(l, 5))
                        tt(bT_lo[:, 0:2, :], lnv[:, :, :], bT_hi[:, 0:2, :].bitcast(f32), ALU.subtract
                           ).then_inc(b_lo.sem, 1)
                        row_max(2)
                        normalise(2)
                    if q == 15:
                        pT_copy(2)
                        merge(14, 0)
                    if q == 16:
                        o_rest(2)
                        row_max(3)
                        merge(14, 1)
                        normalise(3)
                    if q == 17:
                        pT_copy(3)
                        o_rest(3)
                    if q == 18:
                        merge(17, 0)
                        for f in range(2):
                            m_rest(l, f)
                        merge(17, 1)
                        for f in range(2, 4):
                            m_rest(l, f)
                    if q in MIX_ADA[2:]:
                        ada_step(l, 1, MIX_ADA.index(q))
                scaled_y(l, 1, 18, 0, 0)
                split(l, 2, 0)
                read_mods(l, 1)
                scaled_y(l, 1, 19, 0, 1)
                update_x(l, 1)

            def m_rest(l, f):
                kh, t = f // 2, f % 2
                dve.wait_ge(m_hi.sem, m_hi.at(l, f + 1))
                sl = (slice(None), slice(4 * kh, 4 * kh + 4), slice(t * 128, (t + 1) * 128))
                tt(hT_lo[sl], T[f][:].rearrange("p (k n) -> p k n", k=4), hT_hi[sl].bitcast(f32),
                   ALU.subtract).then_inc(m_lo.sem, 1)

            nc.vector.memset(rows[:, :, :], 0.0).then_inc(rows_clear, 1)
            nc.vector.memset(ones[:], 1.0).then_inc(set_up, 1)
            dve.wait_ge(c_ready, 1)
            chain.start(dve, 0)
            chain.credit = 0
            for h in range(4):
                for e in range(2):
                    dve.wait_ge(pro_arrived[2 * h + e], 16)
                    for r in range(4):
                        j = 4 * e + r
                        w = pro_ada[2 * h + e][:, r * 512:(r + 1) * 512]
                        acc = modacc[:, 2 + h, :]
                        if j == 0:
                            ins = tsc(acc, w, c_act[:, 0:1], None, ALU.mult)
                        else:
                            ins = stt(acc, w, c_act[:, j:j + 1], acc, ALU.mult, ALU.add)
                        if j < 7:
                            chain.link(ins)
                ins.then_inc(pro_done, 1)
            dve.wait_ge(pro_filled, 1)
            for l0 in range(L):
                ins = nc.vector.tensor_copy(vec_all[:, l0 * NVC:l0 * NVC + NV], T[l0][:, 0:NV])
                ins = nc.vector.tensor_copy(vec_all[:, l0 * NVC + NV:(l0 + 1) * NVC], T[l0][:, 128:128 + 2 * CW])
            chain.link(ins)
            dve.wait_ge(cols_summed.sem, 1)
            nc.vector.tensor_copy(mods[:], T[2][:, 0:16]).then_inc(mods_read.sem, 1)
            dve.wait_ge(x_arrived, 16)
            dve.sem_inc(x_updated.sem, x_updated.credit)
            dve.sem_inc(lo_done.sem, lo_done.credit)
            dve.sem_inc(ada_done.sem, ada_done.credit)
            chain.credit = chain.n
            with dve.Fori(0, L) as l:
                chain.start(dve, l)
                nc.vector.tensor_copy(vec[:], vec_all[:, ds(l * NVC, NVC)]).then_inc(vec_ready.sem, 1)
                dve.wait_ge(vec_ready.sem, vec_ready.at(l, 1))
                ffn(l, 0)
                mix(l)
                ffn(l, 2)
                assert chain.n == DVE_CHAIN_LAYER, chain.n

        @block.gpsimd
        def _(pool):
            tt = nc.gpsimd.tensor_tensor
            chain = pool_chain
            chain.per_layer = POOL_CHAIN_LAYER

            def rstd(out_ap, in_ap, width, cols, ready, more=()):
                pass_waits(pool, "pool")
                for o, i_, w in ((out_ap, in_ap, width),) + tuple(more):
                    ins = nc.gpsimd.tensor_scalar(o, i_, 1.0 / w, EPS, ALU.mult, ALU.add)
                chain.link(ins)
                whole, n = cols
                tt(whole, whole, minus_half[:, 0:n], ALU.pow).then_inc(ready.sem, 1)

            def enter(l, stage):
                for t in range(2):
                    pool.wait_ge(ssx_ready.sem, ssx_ready.at(l, 2 * stage + t + 1))
                    rstd(rsx[:, t:t + 1], ssx[:, t:t + 1], D, (rsx[:, t:t + 1], 1), rsx_ready)

            def leave(l, stage):
                for t in range(2):
                    pool.wait_ge(ssy_ready.sem, ssy_ready.at(l, 4 * stage + 2 + t + 1))
                    chain.link(tt(ssy[:, t, 0:1], ssy[:, t, 0:1], ssy[:, t, 1:2], ALU.add))
                    rstd(rsy[:, t:t + 1], ssy[:, t, 0:1], D, (rsy[:, t:t + 1], 1), rsy_ready)

            def rotate(dst1, dst2, x1, x2, cos, sin, shape, ready, links):
                n = shape[0] * shape[1]
                view = lambda k: rot[:, k, 0:n].rearrange("p (h d) -> p h d", h=shape[0])
                tt(view(0), x1, cos, ALU.mult)
                tt(view(1), x2, sin, ALU.mult)
                tt(view(2), x1, sin, ALU.mult)
                chain.link(tt(view(3), x2, cos, ALU.mult))
                tt(dst1, view(0), view(1), ALU.subtract)
                ins = tt(dst2, view(2), view(3), ALU.add)
                if ready is None:
                    chain.link(ins)
                else:
                    ins.then_inc(ready.sem, 1)
                    pool.wait_ge(ready.sem, links)

            nc.gpsimd.memset(minus_half[:], -0.5).then_inc(set_up, 1)
            pool.wait_ge(set_up, 2)
            pool.wait_ge(consts_arrived, 80)
            with pool.Fori(0, L) as l:
                chain.start(pool, l)
                enter(l, 0)
                leave(l, 0)
                enter(l, 1)
                for t in range(2):
                    pool.wait_ge(ssa_ready.sem, ssa_ready.at(l, t + 1))
                    rstd(rsa[:, t, 0:1], ssa[:, t, 0:1], QL, (rsa[:, t, :], 2), rsa_ready,
                         more=((rsa[:, t, 1:2], ssa[:, t, 1:2], KVL),))
                pool.wait_ge(q_copied.sem, q_copied.at(l, 4))
                for t in range(2):
                    heads = qf[:, t, :].rearrange("p (h d) -> p h d", h=H)
                    x1, x2 = heads[:, :, NOPE:NOPE + 16], heads[:, :, NOPE + 16:QKD]
                    cos = rope[:, t, 0, :].unsqueeze(1).to_broadcast([128, H, 16])
                    sin = rope[:, t, 1, :].unsqueeze(1).to_broadcast([128, H, 16])
                    rotate(x1, x2, x1, x2, cos, sin, (H, 16), q_rotated, q_rotated.at(l, t + 1))
                for t in range(2):
                    x1, x2 = za[:, t, QL + KVL:QL + KVL + 16], za[:, t, QL + KVL + 16:512]
                    one = lambda a: a.unsqueeze(1)
                    rotate(one(k_rot[:, t, 0:16]), one(k_rot[:, t, 16:32]), one(x1), one(x2),
                           one(rope[:, t, 0, :]), one(rope[:, t, 1, :]), (1, 16), None, None)
                    pass_waits(pool, "pool")
                    nc.gpsimd.tensor_copy(kf[:, t, :].rearrange("p (h d) -> p h d", h=H)[:, :, NOPE:QKD],
                                          k_rot[:, t, :].unsqueeze(1).to_broadcast([128, H, ROPE])
                                          ).then_inc(k_rotated.sem, 1)
                pool.wait_ge(mv_ready.sem, mv_ready.at(l, 1))
                pass_waits(pool, "pool")
                chain.link(nc.gpsimd.tensor_scalar(rsc[:], mv[:, :, 1], 1.0, EPS, ALU.mult, ALU.add))
                tt(rsc[:], rsc[:], minus_half[:, 0:2], ALU.pow).then_inc(rsc_ready.sem, 1)
                leave(l, 1)
                enter(l, 2)
                leave(l, 2)
                assert chain.n == POOL_CHAIN_LAYER, chain.n

        @block.tensor
        def _(pe):
            mm = nc.tensor.matmul

            def transpose(dst, src, rows_):
                return nc.tensor.transpose(dst, src, ident[0:rows_, 0:rows_])

            def product(l, stage, q, xh, xl, segs, i=0, before=None, between=None, operand=None):
                panel, slot, _ = stage_panel(stage, q, i)
                bounds = pieces(stage, q)
                seen = set()
                for s, (pair, blocks, width, starts, ends) in enumerate(segs):
                    for t in range(2):
                        if before is not None:
                            before(s, t)
                        for b, (k, col, parts) in enumerate(blocks):
                            if operand is not None:
                                operand(k, t)
                            last_piece = max(n for n, (_, a, e) in enumerate(bounds)
                                             if a < col + width and e > col)
                            if last_piece not in seen:
                                seen.add(last_piece)
                                pe.wait_ge(lo_done.sem, lo_done.at(l, 4 * panel + last_piece + 1))
                            z = Z[pair][t][:, 0:width]
                            a_hi_ = xh[0:parts, k, t * 128:(t + 1) * 128]
                            a_lo_ = xl[0:parts, k, t * 128:(t + 1) * 128]
                            wh = w_hi[0:parts, slot, col:col + width]
                            wl = w_lo[0:parts, slot, col:col + width]
                            mm(z, a_hi_, wh, start=starts and b == 0, stop=False)
                            mm(z, a_hi_, wl, start=False, stop=False)
                            ins = mm(z, a_lo_, wh, start=False, stop=ends and b == len(blocks) - 1)
                        ins.then_inc(mm_done.sem, 1)
                        if between is not None and s == 0 and t == 0:
                            between()

            def enter(l, stage):
                for t in range(2):
                    pe.wait_ge(xn_ready.sem, xn_ready.at(l, 2 * stage + t + 1))
                    for half in range(2):
                        for k in range(4):
                            c0 = (4 * half + k) * 128
                            ins = transpose(T[2 * t + half][:, k * 128:(k + 1) * 128], tmp[:, t, c0:c0 + 128], 128)
                        ins.then_inc(ht_filled.sem, 1)

            def wide(stage, pair):
                return [(pair, [(k, 512 * k, 128) for k in range(KD)], 512, True, True)]

            def ht_wait(l, stage):
                seen = set()

                def wait(k, t):
                    n = 2 * t + k // 4
                    if n not in seen:
                        seen.add(n)
                        pe.wait_ge(ht_lo.sem, ht_lo.at(l, 4 * stage + n + 1))
                return wait

            def hidden_fill(l, stage, q, i=0):
                if q >= 4:
                    pe.wait_ge(hid_lo_ready.sem, hid_lo_ready.at(l, N_UP * (stage // 2) + q - 3 + 2 * i))
                pe.wait_ge(hid_ready.sem, hid_ready.at(l, 2 * N_UP * (stage // 2) + 2 * (q - 1) + 4 * i))
                for ch in range(2):
                    for t in range(2):
                        ins = transpose(T[q % 2][:, ch * 256 + t * 128:ch * 256 + (t + 1) * 128],
                                        hid[:, q % 2, t, ch * 128:(ch + 1) * 128], 128)
                ins.then_inc(hid_filled.sem, 1)

            def sum_gain(l, stage, banks):
                pe.wait_ge(ada_done.sem, ada_done.at(l, 2 * ADA_STEPS * stage + 8))
                for n in range(2):
                    mm(banks[n][:], ones[:], modacc[:, n, :], start=True, stop=True).then_inc(gain_summed.sem, 1)

            def sum_cols(bank, halves=(2, 3, 4, 5)):
                for n in range(16):
                    ins = mm(bank[:, n:n + 1], modacc[:, halves[n // 4], (n % 4) * 128:(n % 4 + 1) * 128],
                             ones[:, 0:1], start=True, stop=True)
                ins.then_inc(cols_summed.sem, 1)

            def ffn(l, stage):
                enter(l, stage)
                first = ht_wait(l, stage)

                def up(q, i=0):
                    def bank_free(s, t):
                        if q >= 2:
                            pe.wait_ge(hid_ready.sem, hid_ready.at(
                                l, 2 * N_UP * (stage // 2) + 2 * (q - 2) + 4 * i + t + 1))
                    product(l, stage, q, hT_hi, hT_lo, wide(stage, pair_of(stage, q)), i=i, before=bank_free,
                            between=(lambda: hidden_fill(l, stage, q, i)) if q >= 2 else None,
                            operand=first if q < 2 else None)

                for q in range(4):
                    up(q)
                with pe.Fori(0, (N_UP - 5) // 2) as i:
                    for q in (4, 5):
                        up(q, i)
                up(N_UP - 1)
                for q in range(N_UP, FFN_STEPS):
                    blocks = down_blocks(q)
                    segs = []
                    for n in range(2):
                        mine = [(k, 512 * b, 128) for b, (bn, k) in enumerate(blocks) if bn == n]
                        if mine:
                            segs.append((pair_of(stage, N_UP + n), mine, 512, mine[0][0] == 0,
                                         mine[-1][0] == KF - 1))

                    def bank_free(s, t, q=q, blocks=blocks):
                        n = blocks[0][0] + s
                        if (q == N_UP and s == 0) or (q == FFN_GROUPS_SPLIT and s == 1):
                            up_panel = N_UP - 2 + n
                            pe.wait_ge(hid_ready.sem, hid_ready.at(
                                l, 2 * N_UP * (stage // 2) + 2 * up_panel + t + 1))
                    seen = set()

                    def ready(k, t, q=q, seen=seen):
                        if q <= FFN_GROUPS_SPLIT and k // 2 not in seen:
                            seen.add(k // 2)
                            pe.wait_ge(hid_lo_ready.sem, hid_lo_ready.at(l, N_UP * (stage // 2) + k // 2 + 1))
                    product(l, stage, q, hid_hi, hid_lo, segs, before=bank_free,
                            between=(lambda: hidden_fill(l, stage, q)) if q - 2 < N_UP else None, operand=ready)
                    if q == N_UP + 1:
                        sum_gain(l, stage, (T[2], T[3]))
                    if q == FFN_GROUPS_SPLIT:
                        pe.wait_ge(gain_read.sem, gain_read.at(l, 2 * stage + 2))
                        pe.wait_ge(ada_done.sem, ada_done.at(l, 2 * ADA_STEPS * (stage + 1)))
                        sum_cols(T[2])

            def mix(l):
                enter(l, 1)
                first = ht_wait(l, 1)
                w = lambda sig, n: pe.wait_ge(sig.sem, sig.at(l, n))

                def reader(g, t):
                    if g < 0:
                        return
                    if g == 0:
                        w(ssa_ready, t + 1)
                    elif g == 1:
                        w(u_ready, t + 1)
                    elif g < 4:
                        w(zt_copied, 2 * (g - 2) + t + 1)
                    elif g < 6:
                        w(q_copied, 2 * (g - 4) + t + 1)
                    elif g < 8:
                        w(kv_copied, 2 * (g - 6) + t + 1)
                    else:
                        br, part = (g - 8) // 4, (g - 8) % 4
                        if part < 2:
                            w(gate_ready, 4 * br + 2 * part + t + 1)
                        else:
                            w(merged_done, 4 * br + 2 * (part - 2) + t + 1)

                def whole(q, g, xh=hT_hi, xl=hT_lo, between=None, operand=None):
                    product(l, 1, q, xh, xl, wide(1, pair_of(1, g)), before=lambda s, t: reader(g - 2, t),
                            between=between, operand=operand)

                def scores(i):
                    t, hh = i // 2, i % 2
                    for b in range(2):
                        for h in (2 * b, 2 * b + 1):
                            head = 4 * hh + h
                            ins = mm(T[2 + b][:, (h % 2) * 256:(h % 2) * 256 + 256],
                                     qT[0:QKD, head, t * 128:(t + 1) * 128], kT[0:QKD, head, :],
                                     start=True, stop=True)
                        ins.then_inc(scores_done.sem, 1)

                def pT_fill(i):
                    w(p_ready, i + 1)
                    for kc in range(2):
                        for h in range(4):
                            ins = transpose(T[kc][:, h * 128:(h + 1) * 128], p[:, h, kc * 128:(kc + 1) * 128], 128)
                        ins.then_inc(pT_filled.sem, 1)

                def attend(i):
                    w(pT_act, i + 1)
                    w(pT_dve, i + 1)
                    hh = i % 2
                    for h in range(4):
                        head = 4 * hh + h
                        for kc in range(2):
                            ins = mm(T[0][64 * (h % 2):64 * (h % 2) + 64, (h // 2) * 128:(h // 2 + 1) * 128],
                                     v[:, kc, head * VH:(head + 1) * VH], pT[:, kc, h, :],
                                     start=kc == 0, stop=kc == 1)
                    ins.then_inc(o_done.sem, 1)

                def kq_fill(f):
                    src = kf if f < 4 else qf
                    t, hh = (f % 4) // 2, f % 2
                    bank = T[(2, 3, 0, 1)[f % 4]]
                    for h in range(4):
                        c0 = (4 * hh + h) * QKD
                        ins = transpose(bank[0:QKD, h * 128:(h + 1) * 128], src[:, t, c0:c0 + QKD], 128)
                    ins.then_inc(kq_filled.sem, 1)

                def branch(q, g, rows_, between=None):
                    br = next(b for b, s in BRANCH_STEPS.items() if 0 <= q - s < 3)
                    segs = [(pair_of(1, g + n), [(k, k * D + n * 512, 128) for k in range(rows_)], 512, True, True)
                            for n in range(2)]
                    product(l, 1, q, oT_hi if br == 0 else bT_hi, oT_lo if br == 0 else bT_lo, segs,
                            before=lambda s, t: reader(g + s - 2, t), between=between)

                whole(0, 0, operand=first)
                whole(1, 1, operand=first)

                def latent_fill():
                    w(an_ready, 2)
                    for k in range(4):
                        r = QL - 256 if k == 2 else 128
                        c0 = 128 * k if k < 3 else QL
                        for t in range(2):
                            ins = transpose(T[k // 2][0:r, (k % 2) * 256 + t * 128:(k % 2) * 256 + (t + 1) * 128],
                                            za[:, t, c0:c0 + r], 128)
                        if k % 2:
                            ins.then_inc(an_filled.sem, 1)
                whole(2, 2, between=latent_fill)
                w(u_ready, 2)
                for k in range(2):
                    for t in range(2):
                        ins = transpose(T[2][:, k * 256 + t * 128:k * 256 + (t + 1) * 128],
                                        u[:, t, k * 128:(k + 1) * 128], 128)
                ins.then_inc(u_filled.sem, 1)
                whole(3, 3)
                w(zt_copied, 2)
                w(a_lo, 4)
                for g in range(4):
                    bank, c0 = T[g // 2], (g % 2) * 256
                    z = lambda k: zt[:, k, 0, g * 128:(g + 1) * 128]
                    mm(bank[:, c0:c0 + BAND0], z(0), band[:, 0, g, 0:BAND0], start=True, stop=True)
                    mm(bank[:, c0 + BAND0:c0 + BAND], z(0), band[:, 0, g, BAND0:BAND], start=True, stop=False)
                    mm(bank[:, c0 + BAND0:c0 + BAND], z(1), band[:, 1, g, 0:BAND - BAND0], start=False, stop=True)
                    ins = mm(bank[:, c0 + BAND:c0 + S], z(1), band[:, 1, g, BAND - BAND0:BAND],
                             start=True, stop=True)
                    if g % 2:
                        ins.then_inc(pool1_done.sem, 1)
                w(a_lo, 4)
                uq_blocks = lambda c0: [(k, k * H * QKD + c0, 128 if k < 2 else QL - 256) for k in range(3)]
                product(l, 1, UQ, aT_hi, aT_lo,
                        [(pair_of(1, 4), uq_blocks(0), 512, True, True),
                         (pair_of(1, 5), uq_blocks(512), 256, True, True)],
                        before=lambda s, t: reader(2 + s, t))
                w(zt_copied, 4)
                w(uT_ready, 1)
                w(dT_act, 1)
                w(dT_dve, 1)
                for g in range(4):
                    for k in range(2):
                        ins = mm(T[(2, 3, 0, 1)[g]][:], zt[:, k, 1, g * 128:(g + 1) * 128], dft[:, k, :],
                                 start=k == 0, stop=k == 1)
                    ins.then_inc(fnet1_done.sem, 1)
                product(l, 1, UKV, aT_hi, aT_lo,
                        [(pair_of(1, 6 + n), [(3, 512 * n, 128)], 512, True, True) for n in range(2)],
                        before=lambda s, t: reader(4 + s, t))
                w(U_act, 2)
                w(U_dve, 2)
                sum_gain(l, 1, (T[0], T[1]))
                whole(6, 8)
                w(gain_read, 4)
                for b in range(2):
                    for k in range(2):
                        ins = mm(T[b][:].rearrange("p (g n) -> p g n", g=2), chan[:, k, :],
                                 U[:, 2 * b:2 * b + 2, k * 256:(k + 1) * 256], start=k == 0, stop=k == 1)
                    ins.then_inc(fnet2_done.sem, 1)
                w(kv_copied, 4)
                w(k_rotated, 2)
                kq_fill(0)
                kq_fill(1)
                whole(7, 9)
                w(b_lo, 2)
                kq_fill(2)
                kq_fill(3)
                w(q_rotated, 2)
                w(kq_act, 1)
                w(kq_dve, 1)
                kq_fill(4)
                kq_fill(5)
                branch(8, 10, 4)
                w(kq_act, 3)
                w(kq_dve, 3)
                kq_fill(6)
                kq_fill(7)
                scores(0)
                whole(9, 12)
                w(kq_act, 4)
                w(kq_dve, 4)
                pT_fill(0)
                w(poolw_arrived, 16)
                w(exp_done, 1)
                for g in range(4):
                    ins = mm(T[2 + g // 2][:, (g % 2) * 256:(g % 2) * 256 + 256], poolw[:, g, :], dT[:, g, :],
                             start=True, stop=True)
                    if g % 2:
                        ins.then_inc(pool2_done.sem, 1)
                whole(10, 13)
                attend(0)
                w(b_lo, 4)
                scores(1)
                w(yc_ready, 1)
                for k in range(2):
                    for t in range(2):
                        ins = transpose(T[1][:, t * 256 + k * 128:t * 256 + (k + 1) * 128],
                                        yc[:, k, t * 128:(t + 1) * 128], 128)
                ins.then_inc(yc_filled.sem, 1)
                branch(11, 14, 4)
                w(o_lo, 1)
                w(lnx_ready, 1)
                pT_fill(1)
                whole(12, 16)
                attend(1)
                w(lnx_ready, 1)
                for t in range(2):
                    for k in range(2):
                        ins = transpose(T[1][:, k * 256 + t * 128:k * 256 + (t + 1) * 128],
                                        lnx[:, t, k * 128:(k + 1) * 128], 128)
                ins.then_inc(lnx_filled.sem, 1)
                w(exp_done, 2)
                scores(2)
                whole(13, 17)
                w(o_lo, 2)
                w(lnv_ready, 1)
                pT_fill(2)
                w(b_lo, 5)
                branch(14, 18, 2)
                attend(2)
                w(exp_done, 3)
                scores(3)
                whole(15, 20)
                w(o_lo, 3)
                pT_fill(3)
                whole(16, 21, between=lambda: attend(3))
                w(o_lo, 4)
                branch(17, 22, 4)
                for f in range(4):
                    kh, t = f // 2, f % 2
                    w(merged_done, 12 + f + 1)
                    for k in range(4):
                        c0 = (4 * kh + k) * 128
                        ins = transpose(T[f][:, k * 128:(k + 1) * 128], tmp[:, t, c0:c0 + 128], 128)
                    ins.then_inc(m_filled.sem, 1)
                seen = set()

                def merged_ready(k, t):
                    n = 2 * (k // 4) + t
                    if n not in seen:
                        seen.add(n)
                        w(m_lo, n + 1)
                whole(18, 24, operand=merged_ready)
                pe.wait_ge(ada_done.sem, ada_done.at(l, 4 * ADA_STEPS))
                sum_cols(T[0], halves=(2, 3, 0, 1))
                whole(19, 25)

            pe.wait_ge(vrows_arrived, 24 * 16)
            pe.wait_ge(consts_arrived, 80)
            pe.wait_ge(set_up, 2)
            for l0 in range(L):
                transpose(T[l0][:, 0:NV], rows[0:NV, l0, :], NV)
                ins = transpose(T[l0][:, 128:128 + 2 * CW], crows[:, l0, :], 2 * CW)
            ins.then_inc(pro_filled, 1)
            pe.wait_ge(pro_done, 4)
            sum_cols(T[2])
            pe.sem_inc(mm_done.sem, mm_done.credit)
            with pe.Fori(0, L) as l:
                ffn(l, 0)
                mix(l)
                ffn(l, 2)


DVE_CHAIN_LAYER = 131
POOL_CHAIN_LAYER = 27
LOOP_LINKS = 4

_INS = ["x", "c", "ada_w", "ada_b", "norm_g", "ffn1_w_in", "ffn1_w_out", "ffn2_w_in", "ffn2_w_out",
        "w_in", "q_norm_g", "w_uq", "kv_norm_g", "w_ukv", "w_a", "conv_w", "conv_b", "conv_ln_g",
        "conv_ln_b", "w_b", "pool_w", "pool_scale", "w_c", "w_d", "w_out"]


def shape_constants():
    import numpy as np

    ident = np.eye(128, dtype=np.float32)
    t = np.arange(S)
    angle = 2 * np.pi * np.outer(t, t) / S
    norm = (S * 128) ** -0.5
    dft = np.concatenate([np.cos(angle), np.sin(angle)], axis=1) * norm
    ch = np.arange(128)
    angle = 2 * np.pi * np.outer(ch, ch) / 128
    chan = np.concatenate([np.cos(angle), -np.sin(angle)], axis=1)
    full = np.zeros((len(WINDOWS), S, S))
    for g, w in enumerate(WINDOWS):
        lo = w // 2
        for s in range(S):
            a, b = max(s - lo, 0), min(s + w - lo, S)
            full[g, a:b, s] = 1.0 / (b - a)
            full[g, s, s] -= 1.0
    band = np.zeros((128, 2, len(WINDOWS), BAND))
    for g in range(len(WINDOWS)):
        band[:, 0, g, :] = full[g, 0:128, 0:BAND]
        band[:, 1, g, :] = full[g, 128:256, BAND0:S]
    inv = np.float32(10000.0) ** (-np.arange(0, ROPE, 2, dtype=np.float32) / np.float32(ROPE))
    ang = (t.astype(np.float32)[:, None] * inv[None, :]).astype(np.float64)
    rope = np.stack([np.cos(ang), np.sin(ang)], axis=1)
    return [("ident_c", ident), ("dft_c", dft), ("chan_c", chan), ("band_c", band), ("rope_c", rope)]


def kernel(**inputs):
    import numpy as np
    import concourse.bacc as bacc
    from concourse.bass_utils import run_bass_kernel_spmd

    nc = bacc.Bacc("TRN2", target_bir_lowering=False, num_devices=1, dynamic_dma_scratch_size=256)
    arrays, args = {}, []
    named = [(n, np.ascontiguousarray(inputs[n])) for n in _INS]
    named += [(n, np.ascontiguousarray(a, dtype=np.float32)) for n, a in shape_constants()]
    for name, a in named:
        arrays[f"in_{name}"] = a
        args.append(nc.dram_tensor(f"in_{name}", a.shape, mybir.dt.from_np(a.dtype), kind="ExternalInput").ap())
    args.append(nc.dram_tensor("out_0", (1, S, D), mybir.dt.float32, kind="ExternalOutput").ap())
    build(nc, *args)
    r = run_bass_kernel_spmd(nc, [arrays], core_ids=[0])
    return r.results[0]["out_0"]
```

```python
import concourse.bass as bass
from concourse import mybir
from contextlib import ExitStack

D = 1024
S = 256
L = 2
FF = 2816
H = 8
QL = 352
KVL = 128
NOPE = 64
ROPE = 32
VH = 64
QKD = NOPE + ROPE
CW = 31
CC = 256
WINDOWS = (2, 4, 8, 16)
EPS = 1e-6
P128 = 128
KD = D // P128
KF = FF // P128
UPW = 256
N_UP = FF // UPW
N_DOWN = 6
MIX = 2048
BAND = 136
BAND0 = 120

FFN_STEPS = N_UP + N_DOWN
MIX_STEPS = 20
PANELS = 2 * FFN_STEPS + MIX_STEPS
STAGE_PANEL = (0, FFN_STEPS, FFN_STEPS + MIX_STEPS)
STAGE_GROUP = (0, 13, 39)
UQ, UKV = 4, 5
BRANCH_STEPS = {3: 6, 2: 9, 1: 12, 0: 15}
ADA_STEPS = 12
ADA_FIRST = 2
MIX_ADA = (1, 2, 3, 4, 9, 11, 12, 13, 15, 16, 17, 18)

FFN_GROUPS_SPLIT = N_UP + 3


def segments(panel):
    if panel < 0:
        panel += PANELS
    for s in (0, 2):
        q = panel - STAGE_PANEL[s]
        if 0 <= q < FFN_STEPS:
            return 2 if q == FFN_GROUPS_SPLIT else 1
    q = panel - STAGE_PANEL[1]
    return 2 if q in (UQ, UKV, 8, 11, 14, 17) else 1


MM_BEFORE = [0]
for _p in range(PANELS):
    MM_BEFORE.append(MM_BEFORE[-1] + 2 * segments(_p))
MM_LAYER = MM_BEFORE[-1]


def build(nc, x, c, ada_w, ada_b, norm_g, ffn1_w_in, ffn1_w_out, ffn2_w_in, ffn2_w_out, w_in,
          q_norm_g, w_uq, kv_norm_g, w_ukv, w_a, conv_w, conv_b, conv_ln_g, conv_ln_b, w_b,
          pool_w, pool_scale, w_c, w_d, w_out, ident_c, dft_c, chan_c, band_c, rope_c, out):
    f32 = mybir.dt.float32
    f32r = mybir.dt.float32r
    ALU = mybir.AluOpType
    ACT = mybir.ActivationFunctionType
    AX = mybir.AxisListType
    ds = bass.ds

    ctx = ExitStack()
    with ctx:
        place = [(nc.sbuf_base + 31) // 32 * 32]

        def at(name, shape, offset, dt=f32):
            return nc.alloc_sbuf_tensor_at(name, shape, dt, offset=offset)

        def sb(name, shape, dt=f32):
            n = 4
            for s in shape[1:]:
                n *= s
            off = place[0]
            place[0] += (n + 31) // 32 * 32
            return at(name, shape, off, dt)

        raw = sb("raw", [128, 2, 4096])
        rings = place[0]
        w_hi = sb("w_hi", [128, 2, 4096], f32r)
        w_lo = sb("w_lo", [128, 2, 4096], f32r)
        ada = sb("ada", [128, 2, 2, 512])
        xs = sb("xs", [128, 2, D])
        hT_hi = sb("hT_hi", [128, KD, S], f32r)
        hT_lo = sb("hT_lo", [128, KD, S], f32r)
        modacc_at = place[0]
        modacc = sb("modacc", [128, 6, 512])
        gain = sb("gain", [128, D])
        tmp = sb("tmp", [128, 2, D])
        dft = sb("dft", [128, 2, 512])
        band = sb("band", [128, 2, 4, BAND])
        chan = sb("chan", [128, 2, 128])
        ident = sb("ident", [128, 128])
        ones = sb("ones", [128, 128])
        rope = sb("rope", [128, 2, 2, 16])
        NV = 110
        NVC = NV + 2 * CW
        vec = sb("vec", [128, NVC])
        vec_next = sb("vec_next", [128, L * NVC])
        poolw = sb("poolw", [128, 4, 128])
        c_raw = sb("c_raw", [128, 8])
        c_act = sb("c_act", [128, 8])
        ab = sb("ab", [128, 3, 8])
        minus_half = sb("minus_half", [128, 4])
        ssx = sb("ssx", [128, 2])
        rsx = sb("rsx", [128, 2])
        ssy = sb("ssy", [128, 2, 2])
        rsy = sb("rsy", [128, 2])
        ssa = sb("ssa", [128, 2, 2])
        rsa = sb("rsa", [128, 2, 2])
        k_rot = sb("k_rot", [128, 2, ROPE])
        bns = sb("bns", [128, 2, 6])
        mv = sb("mv", [128, 2, 2])
        rsc = sb("rsc", [128, 2])
        mx = sb("mx", [128, 4])
        nmx = sb("nmx", [128, 4])
        rs = sb("rs", [128, 4])
        rinv = sb("rinv", [128, 4])
        arena = place[0]
        assert arena + 55552 <= nc.sbuf_usable_end, (arena + 55552, nc.sbuf_usable_end)

        hid_hi = at("hid_hi", [128, KF, S], arena, f32r)
        hid_lo = at("hid_lo", [128, KF, S], arena + 22528, f32r)
        hid = at("hid", [128, 2, 2, UPW], arena + 45056)
        junk = at("junk", [128, D], arena + 45056)
        kT = at("kT", [128, H, S], arena)
        U = at("U", [128, 4, 512], arena)
        qT = at("qT", [128, H, S], arena + 8192)
        kf = at("kf", [128, 2, H * QKD], arena + 8192)
        zt = at("zt", [128, 2, 2, 512], arena + 16384)
        gates = at("gates", [128, 2, D], arena + 16384)
        aT_hi = at("aT_hi", [128, 4, S], arena + 24576, f32r)
        za = at("za", [128, 2, 512], arena + 28672)
        bT_hi = at("bT_hi", [128, 4, S], arena + 24576, f32r)
        bT_lo = at("bT_lo", [128, 4, S], arena + 28672, f32r)
        qf = at("qf", [128, 2, H * QKD], arena + 32768)
        oT_hi = at("oT_hi", [128, 4, S], arena + 32768, f32r)
        oT_lo = at("oT_lo", [128, 4, S], arena + 36864, f32r)
        rot = at("rot", [128, 4, 128], arena + 38912)
        dT = at("dT", [128, 4, S], arena + 40960)
        pT = at("pT", [128, 2, 4, 128], arena + 40960)
        aT_lo = at("aT_lo", [128, 4, S], arena + 45056, f32r)
        p = at("p", [128, 4, S], arena + 45056)
        PADW = S + CW - 1
        uT = at("uT", [128, 2, PADW], arena + 49152)
        lnv = at("lnv", [128, 2, S], arena + 49152)
        yc = at("yc", [128, 2, S], arena + 51456)
        lnx = at("lnx", [128, 2, CC], arena + 51456)
        u = at("u", [128, 2, CC], arena + 53504)
        sgv = at("sgv", [128, 2, S], arena + 53504)
        v = at("v", [128, 2, H * VH], modacc_at + 8192)
        pro_ada = [at(f"pro_ada{i}", [128, 2048], arena + 8192 * i if i < 4 else rings + 32768 + 8192 * (i - 4))
                   for i in range(8)]
        rows = at("rows", [128, L, 128], arena + 40960)
        crows = at("crows", [2 * CW, L, 128], arena + 41984)

        Z = [[ctx.enter_context(nc.psum_tensor(f"Z{i}{j}", [128, 512], f32)) for j in range(2)] for i in range(2)]
        T = [ctx.enter_context(nc.psum_tensor(f"T{i}", [128, 512], f32)) for i in range(4)]

        V_G, V_B, V_CB, V_LG, V_LB, V_PS, V_QG, V_KG, V_CW = 0, 24, 96, 98, 100, 102, 106, 109, 110

        class Signal:

            def __init__(self, name, per_layer, credit=0):
                self.sem = ctx.enter_context(nc.semaphore(name))
                self.per_layer, self.credit = per_layer, credit

            def at(self, l, n):
                return l * self.per_layer + n + self.credit

        class Chain(Signal):

            def start(self, eng, l):
                self.eng, self.l, self.n, self.extra = eng, l, 0, 0

            def link(self, ins):
                ins.then_inc(self.sem, 1)
                self.n += 1
                self.eng.wait_ge(self.sem, self.at(self.l, self.n) + self.extra)

        raw_arrived = [[Signal(f"raw_arrived{s}{part}", PANELS // 2 * 16 + (16 if s == 0 else 0))
                        for part in range(2)] for s in range(2)]
        hi_done = Signal("hi_done", 4 * PANELS)
        lo_done = Signal("lo_done", 4 * PANELS, credit=8)
        mm_done = Signal("mm_done", MM_LAYER, credit=4)
        ada_arrived = [Signal(f"ada_arrived{s}", 3 * ADA_STEPS * 16) for s in range(2)]
        ada_done = Signal("ada_done", 6 * ADA_STEPS, credit=2)
        x_updated = Signal("x_updated", 6, credit=2)
        ssx_ready = Signal("ssx_ready", 6)
        rsx_ready = Signal("rsx_ready", 6)
        xn_ready = Signal("xn_ready", 6)
        ht_filled = Signal("ht_filled", 12)
        hf_act = Signal("hf_act", 6)
        hf_dve = Signal("hf_dve", 6)
        ht_hi = Signal("ht_hi", 12)
        ht_lo = Signal("ht_lo", 12)
        ab_ready = Signal("ab_ready", 6)
        ssy_ready = Signal("ssy_ready", 12)
        y_scaled = Signal("y_scaled", 12)
        rsy_ready = Signal("rsy_ready", 6)
        silu_ready = Signal("silu_ready", 4 * N_UP)
        hid_ready = Signal("hid_ready", 4 * N_UP)
        hid_filled = Signal("hid_filled", 2 * N_UP)
        hid_hi_ready = Signal("hid_hi_ready", 2 * N_UP)
        hid_lo_ready = Signal("hid_lo_ready", 2 * N_UP)
        rows_arrived = Signal("rows_arrived", 96)
        gain_summed = Signal("gain_summed", 6)
        gain_read = Signal("gain_read", 6)
        cols_summed = Signal("cols_summed", 6)
        za_copied = Signal("za_copied", 2)
        ssa_ready = Signal("ssa_ready", 2)
        rsa_ready = Signal("rsa_ready", 2)
        an_ready = Signal("an_ready", 2)
        an_filled = Signal("an_filled", 2)
        a_hi = Signal("a_hi", 4)
        a_lo = Signal("a_lo", 4)
        sgb_ready = Signal("sgb_ready", 2)
        u_ready = Signal("u_ready", 2)
        u_filled = Signal("u_filled", 1)
        uT_ready = Signal("uT_ready", 1)
        zt_copied = Signal("zt_copied", 4)
        pool1_done = Signal("pool1_done", 2)
        dT_act = Signal("dT_act", 1)
        dT_dve = Signal("dT_dve", 1)
        pool2_done = Signal("pool2_done", 2)
        fnet1_done = Signal("fnet1_done", 4)
        U_act = Signal("U_act", 2)
        U_dve = Signal("U_dve", 2)
        fnet2_done = Signal("fnet2_done", 2)
        b_hi = Signal("b_hi", 2 + 2 + 1)
        b_lo = Signal("b_lo", 2 + 2 + 1)
        q_copied = Signal("q_copied", 4)
        kv_copied = Signal("kv_copied", 4)
        k_rotated = Signal("k_rotated", 2)
        q_rotated = Signal("q_rotated", 2)
        kq_filled = Signal("kq_filled", 8)
        kq_act = Signal("kq_act", 4)
        kq_dve = Signal("kq_dve", 4)
        scores_done = Signal("scores_done", 8)
        nmx_ready = Signal("nmx_ready", 4)
        exp_done = Signal("exp_done", 4)
        p_ready = Signal("p_ready", 4)
        pT_filled = Signal("pT_filled", 8)
        pT_act = Signal("pT_act", 4)
        pT_dve = Signal("pT_dve", 4)
        o_done = Signal("o_done", 4)
        o_hi = Signal("o_hi", 4)
        o_lo = Signal("o_lo", 4)
        yc_ready = Signal("yc_ready", 1)
        yc_filled = Signal("yc_filled", 1)
        mv_ready = Signal("mv_ready", 1)
        rsc_ready = Signal("rsc_ready", 1)
        lnx_ready = Signal("lnx_ready", 1)
        lnx_filled = Signal("lnx_filled", 1)
        sgv_ready = Signal("sgv_ready", 1)
        lnv_ready = Signal("lnv_ready", 1)
        gate_ready = Signal("gate_ready", 16)
        merged_done = Signal("merged_done", 16)
        m_filled = Signal("m_filled", 4)
        m_hi = Signal("m_hi", 4)
        m_lo = Signal("m_lo", 4)
        vec_ready = Signal("vec_ready", 1)
        poolw_arrived = Signal("poolw_arrived", 16)
        c_arrived = ctx.enter_context(nc.semaphore("c_arrived"))
        x_arrived = [ctx.enter_context(nc.semaphore(f"x_arrived{t}")) for t in range(2)]
        vrows_arrived = ctx.enter_context(nc.semaphore("vrows_arrived"))
        ident_arrived = ctx.enter_context(nc.semaphore("ident_arrived"))
        consts_arrived = ctx.enter_context(nc.semaphore("consts_arrived"))
        pro_arrived = [ctx.enter_context(nc.semaphore(f"pro_arrived{i}")) for i in range(8)]
        set_up = ctx.enter_context(nc.semaphore("set_up"))
        rows_clear = ctx.enter_context(nc.semaphore("rows_clear"))
        c_ready = ctx.enter_context(nc.semaphore("c_ready"))
        pro_done = ctx.enter_context(nc.semaphore("pro_done"))
        pro_filled = ctx.enter_context(nc.semaphore("pro_filled"))
        out_stored = ctx.enter_context(nc.semaphore("out_stored"))
        passed = {e: ctx.enter_context(nc.semaphore(f"passed_{e}")) for e in ("dve", "pool")}

        def pass_waits(eng, e):
            eng.sem_inc(passed[e], 1)

        dve_chain = Chain("dve_chain", 0)
        act_chain = Chain("act_chain", 0)
        pool_chain = Chain("pool_chain", 0)

        def stage_panel(stage, q, i=0):
            b = STAGE_PANEL[stage] + q
            return b + 2 * i, b % 2, b // 2 + i

        def down_blocks(q):
            j = q - N_UP
            return [(b // KF, b % KF) for b in range(max(8 * j - 4, 0), 8 * j + 4)]

        def pieces(stage, q):
            if stage != 1:
                width = 512 if q == N_UP else 1024
            elif q == UQ:
                return [(128, 0, 384), (128, 384, 768), (128, 768, 1536), (QL - 256, 1536, 2304)]
            elif q == UKV:
                width = 256
            else:
                width = 512 if q == BRANCH_STEPS[1] + 2 else 1024
            return [(128, i * width, (i + 1) * width) for i in range(4)]

        def second_part(stage, q):
            if stage != 1:
                return 0 if 0 < q + stage and q < N_UP else 1 if q == FFN_GROUPS_SPLIT else 2
            return 3 if q == UQ else 2

        def mm_after(panel, seg=None, tok=1):
            if seg is None:
                seg = segments(panel) - 1
            return MM_BEFORE[panel] + 2 * seg + tok + 1

        def mm_group(stage, q, seg=0, tok=1):
            return mm_after(STAGE_PANEL[stage] + q, seg, tok)

        def pair_of(stage, g):
            return (STAGE_GROUP[stage] + g) % 2

        PRO_ORDER = (0, 2, 1, 3)

        block = ctx.enter_context(nc.Block())

        @block.sync
        def _(sp):
            sp.dma_start(c_raw[:], c.rearrange("b (p j) -> p (b j)", j=8)).then_inc(c_arrived, 16)
            ada_rows = ada_w.rearrange("l (p j) n -> p l j n", j=8)
            vectors = [(V_G + 8 * s, norm_g[:, 2 * s, :]) for s in range(3)]
            vectors += [(V_B, ada_b), (V_CB, conv_b), (V_LG, conv_ln_g), (V_LB, conv_ln_b), (V_PS, pool_scale),
                        (V_QG, q_norm_g[:, 0:256]), (V_KG, kv_norm_g)]
            for order, h in enumerate(PRO_ORDER):
                for e in range(2):
                    if order == 1:
                        if e == 0:
                            sp.wait_ge(rows_clear, 1)
                        for r, src in vectors[5 * e:5 * e + 5]:
                            n = src.shape[1] // 128
                            sp.dma_start(rows[r:r + n, :, :], src.rearrange("l (k p) -> k l p", p=128)
                                         ).then_inc(vrows_arrived, 16)
                        if e == 0:
                            sp.dma_start(rows[V_QG + 2:V_QG + 3, :, 0:QL - 256],
                                         q_norm_g[:, 256:QL].rearrange("(o l) n -> o l n", o=1)
                                         ).then_inc(vrows_arrived, 16)
                            sp.dma_start(ident[:], ident_c).then_inc(ident_arrived, 16)
                        else:
                            sp.dma_start(crows[:, :, :], conv_w.rearrange("l t (k p) -> (t k) l p", p=128)
                                         ).then_inc(vrows_arrived, 16)
                    if (order, e) in ((2, 0), (3, 1)):
                        t = order - 2
                        sp.dma_start(xs[:, t, :], x[0, t * 128:(t + 1) * 128, :]).then_inc(x_arrived[t], 16)
                    sp.dma_start(pro_ada[2 * h + e][:].rearrange("p (o j n) -> p o j n", o=1, j=4),
                                 ada_rows[:, 0:1, 4 * e:4 * e + 4, 512 * h:512 * h + 512]
                                 ).then_inc(pro_arrived[2 * h + e], 16)

            big = {0: (ffn1_w_in, ffn1_w_out), 2: (ffn2_w_in, ffn2_w_out)}
            kview = lambda w: w.rearrange("l (k p) n -> p l k n", p=128)

            def load_blocks(slot, part, first, w, l, k0, k1, col, n, parts=128):
                dst = raw[0:parts, slot, first:first + (k1 - k0) * n]
                sp.dma_start(dst.rearrange("p (o k n) -> p o k n", o=1, k=k1 - k0),
                             w[0:parts, ds(l, 1), k0:k1, ds(col, n)]).then_inc(raw_arrived[slot][part].sem, 16)

            def wait_raw_slot(l, stage, q, i):
                panel, slot, _ = stage_panel(stage, q, i)
                sp.wait_ge(lo_done.sem, lo_done.at(l, 4 * (panel - 1)))
                return slot

            def load_ada(l, stage, q, i):
                half = q // 2 + i
                for e in range(2):
                    sp.wait_ge(ada_done.sem, ada_done.at(l, 2 * (ADA_STEPS * stage + q + 2 * i) + e - 1))
                    j0 = 4 * (q % 2) + 2 * e
                    if stage == 1:
                        lw, col = ds(l, 1), 5 * D + 512 * half
                    elif q >= 8:
                        lw, col = ds(l, 1), (3 * stage + 2) * D + 512 * (half - 4)
                    elif stage == 0:
                        lw, col = ds(l, 1), 3 * D + 512 * half
                    else:
                        lw, col = slice(L - 1, L), 512 * half
                    src = ada_rows[:, lw, j0:j0 + 2, ds(col, 512)]
                    sp.dma_start(ada[:, e:e + 1, :, :], src).then_inc(ada_arrived[e].sem, 16)

            def load_up(l, stage, q, i=0):
                slot = wait_raw_slot(l, stage, q, i)
                w = kview(big[stage][0])
                view = raw[:, slot, :].rearrange("p (o k n) -> p o k n", o=1, k=KD)
                first = stage == 0 and q == 0
                for ks in (slice(0, KD // 2), slice(KD // 2, KD)) if first else (slice(0, KD),):
                    for g in range(2):
                        part = ks.start * 2 // KD if first else g
                        sp.dma_start(view[:, :, ks, g * UPW:(g + 1) * UPW],
                                     w[:, ds(l, 1), ks, ds(g * FF + UPW * (q + 2 * i), UPW)]
                                     ).then_inc(raw_arrived[slot][part].sem, 16)

            def load_rows(l, stage):
                sp.wait_ge(ht_lo.sem, ht_lo.at(l, 4 * stage + 4))
                g = norm_g.rearrange("l s n -> (l s) n")[ds(l * 6 + 2 * stage + 1, 1), :]
                b = ada_b.rearrange("l (m n) -> (l m) n", n=D)[ds(l * 9 + 3 * stage + 2, 1), :]
                sp.dma_start(gain[:], g.to_broadcast([128, D])).then_inc(rows_arrived.sem, 16)
                sp.dma_start(tmp[:, 0, :], b.to_broadcast([128, D])).then_inc(rows_arrived.sem, 16)

            def ffn(l, stage):
                for q in range(4):
                    load_up(l, stage, q)
                    if q >= ADA_FIRST:
                        load_ada(l, stage, q - ADA_FIRST, 0)
                load_rows(l, stage)
                with sp.Fori(0, (N_UP - 5) // 2) as i:
                    for q in (4, 5):
                        load_up(l, stage, q, i)
                        load_ada(l, stage, q - ADA_FIRST, i)
                load_up(l, stage, N_UP - 1)
                load_ada(l, stage, N_UP - 1 - ADA_FIRST, 0)
                for q in range(N_UP, FFN_STEPS):
                    slot = wait_raw_slot(l, stage, q, 0)
                    blocks = down_blocks(q)
                    half = len(blocks) // 2
                    cut = half
                    for b in range(1, len(blocks)):
                        if blocks[b][0] != blocks[b - 1][0]:
                            cut = b
                    w = kview(big[stage][1])
                    for part, (b0, b1) in enumerate(((0, cut), (cut, len(blocks)))):
                        n, k = blocks[b0]
                        load_blocks(slot, part, b0 * 512, w, l, k, k + b1 - b0, n * 512, 512)
                    if q < ADA_STEPS + ADA_FIRST:
                        load_ada(l, stage, q - ADA_FIRST, 0)

            def mix(l):
                win = kview(w_in)
                for q in range(MIX_STEPS):
                    slot = wait_raw_slot(l, 1, q, 0)
                    if q == UQ:
                        w = w_uq.rearrange("l k n -> k l n")
                        w2 = w_uq[:, 0:256, :].rearrange("l (k p) n -> p l k n", p=128)
                        load_blocks(slot, 0, 0, w2, l, 0, 2, 0, H * QKD)
                        dst = raw[0:QL - 256, slot, 1536:2304].rearrange("p (o n) -> p o n", o=1)
                        sp.dma_start(dst, w[256:QL, ds(l, 1), :]).then_inc(raw_arrived[slot][1].sem, 16)
                    elif q == UKV:
                        for n in range(2):
                            load_blocks(slot, n, 512 * n, kview(w_ukv), l, 0, 1, 512 * n, 512)
                    elif q >= 18:
                        for k in (0, 4):
                            load_blocks(slot, k // 4, 512 * k, kview(w_out), l, k, k + 4, 512 * (q - 18), 512)
                    elif q < 4:
                        for k in (0, 4):
                            load_blocks(slot, k // 4, 512 * k, win, l, k, k + 4, 512 * q, 512)
                    else:
                        br, part = next((b, q - s) for b, s in BRANCH_STEPS.items() if 0 <= q - s < 3)
                        if part < 2:
                            for k in (0, 4):
                                load_blocks(slot, k // 4, 512 * k, win, l, k, k + 4, MIX + br * D + 512 * part, 512)
                        else:
                            w = kview((w_a, w_b, w_c, w_d)[br])
                            step = w.shape[2] // 2
                            for k in range(2):
                                load_blocks(slot, k, k * step * D, w, l, k * step, (k + 1) * step, 0, D)
                    if q - 1 in MIX_ADA:
                        load_ada(l, 1, MIX_ADA.index(q - 1), 0)
                    if q == 3:
                        load_rows(l, 1)
                        sp.dma_start(poolw[:].rearrange("p (o g) n -> p o g n", o=1),
                                     pool_w.rearrange("l g c d -> c l g d")[:, ds(l, 1), :, :]
                                     ).then_inc(poolw_arrived.sem, 16)

            with sp.Fori(0, L) as l:
                ffn(l, 0)
                mix(l)
                ffn(l, 2)
            for t in range(2):
                sp.wait_ge(x_updated.sem, x_updated.at(L, t - 1))
                sp.dma_start(out[0, t * 128:(t + 1) * 128, :], xs[:, t, :]).then_inc(out_stored, 16)
            sp.wait_ge(out_stored, 32)

        @block.scalar
        def _(act):
            copy = lambda o, i: nc.scalar.activation(o, i, ACT.Copy)

            act.wait_ge(c_arrived, 16)
            nc.scalar.activation(c_act[:], c_raw[:], ACT.Silu).then_inc(c_ready, 1)
            act.wait_ge(x_arrived[0], 16)
            nc.scalar.activation(junk[:], xs[:, 0, :], ACT.Square, accum_out=ssx[:, 0:1]
                                 ).then_inc(ssx_ready.sem, 1)
            def split(l, stage, q, i=0, quarters=range(4)):
                panel, slot, visit = stage_panel(stage, q, i)
                before = MM_BEFORE[STAGE_PANEL[stage] + q - 1] if STAGE_PANEL[stage] + q >= 1 \
                    else -2 * segments(-1)
                act.wait_ge(mm_done.sem, mm_done.at(l, before + 4 * i))
                for n in quarters:
                    for part in range(2):
                        if n == max(quarters[0], part * second_part(stage, q)):
                            arrived = raw_arrived[slot][part]
                            act.wait_ge(arrived.sem, arrived.at(l, 16 * (visit + 2 - slot)))
                    parts, a, b = pieces(stage, q)[n]
                    copy(w_hi[0:parts, slot, a:b], raw[0:parts, slot, a:b]).then_inc(hi_done.sem, 1)

            def enter(l, stage):
                def modulated(t):
                    act.wait_ge(ab_ready.sem, ab_ready.at(l, 2 * stage + 1))
                    act.wait_ge(ht_filled.sem, ht_filled.at(l, 4 * stage + 2 * t + 1))
                    for k in range(4):
                        ins = nc.scalar.activation(tmp[:, t, k * 128:(k + 1) * 128],
                                                   T[2 * t][:, k * 128:(k + 1) * 128], ACT.Identity,
                                                   scale=ab[:, 2, k:k + 1], bias=ab[:, 0, k:k + 1])
                    ins.then_inc(hf_act.sem, 1)

                def hi(t, half):
                    w = hf_act if half == 0 else hf_dve
                    act.wait_ge(w.sem, w.at(l, 2 * stage + t + 1))
                    copy(hT_hi[:, 4 * half:4 * half + 4, t * 128:(t + 1) * 128],
                         tmp[:, t, half * 512:(half + 1) * 512].rearrange("p (k n) -> p k n", k=4)
                         ).then_inc(ht_hi.sem, 1)

                if stage == 0:
                    split(l, 0, 0, quarters=(0,))
                modulated(0)
                hi(0, 0)
                act.wait_ge(x_updated.sem, x_updated.at(l, 2 * stage))
                act.wait_ge(ssx_ready.sem, ssx_ready.at(l, 2 * stage + 1))
                nc.scalar.activation(junk[:], xs[:, 1, :], ACT.Square,
                                     accum_out=ssx[:, 1:2]).then_inc(ssx_ready.sem, 1)
                if stage == 0:
                    split(l, 0, 0, quarters=(1,))
                hi(0, 1)
                if stage == 0:
                    split(l, 0, 0, quarters=(2, 3))
                else:
                    split(l, stage, 1, quarters=(0,))
                modulated(1)
                hi(1, 0)
                hi(1, 1)

            def squares_of_y(l, stage, q, n, t):
                act.wait_ge(mm_done.sem, mm_done.at(l, mm_group(stage, q, 0, t)))
                g = (N_UP if stage != 1 else 24) + n
                nc.scalar.activation(junk[:, 0:512], Z[pair_of(stage, g)][t][:], ACT.Square,
                                     accum_out=ssy[:, t, n:n + 1]).then_inc(ssy_ready.sem, 1)

            def leave_first(l, stage, q):
                for t in range(2):
                    if t:
                        act.wait_ge(ssy_ready.sem, ssy_ready.at(l, 4 * stage + t))
                    squares_of_y(l, stage, q, 0, t)

            def leave(l, stage, q):
                act.wait_ge(ssy_ready.sem, ssy_ready.at(l, 4 * stage + 2))
                squares_of_y(l, stage, q, 1, 0)
                act.wait_ge(x_updated.sem, x_updated.at(l, 2 * stage + 1))
                nc.scalar.activation(junk[:], xs[:, 0, :], ACT.Square,
                                     accum_out=ssx[:, 0:1]).then_inc(ssx_ready.sem, 1)
                act.wait_ge(ssx_ready.sem, ssx_ready.at(l, 2 * stage + 3))
                squares_of_y(l, stage, q, 1, 1)

            def silu(l, stage, q, i=0):
                par = pair_of(stage, q)
                hp = q % 2
                if q >= 4:
                    act.wait_ge(hid_filled.sem, hid_filled.at(l, N_UP * (stage // 2) + q - 3 + 2 * i))
                for t in range(2):
                    act.wait_ge(mm_done.sem, mm_done.at(l, mm_group(stage, q - 2, 0, t) + 4 * i))
                    nc.scalar.activation(hid[:, hp, t, :], Z[par][t][:, 0:UPW], ACT.Silu
                                         ).then_inc(silu_ready.sem, 1)

            def hidden_hi(l, stage, q, i=0):
                act.wait_ge(hid_filled.sem, hid_filled.at(l, N_UP * (stage // 2) + q - 2 + 2 * i))
                chunk = hid_hi[:, :, :].rearrange("p k n -> p (k n)")[:, ds((q - 3 + 2 * i) * 512, 512)]
                copy(chunk, T[(q - 3) % 2][:]).then_inc(hid_hi_ready.sem, 1)

            def ffn(l, stage):
                enter_split(l, stage)
                for q in range(2, 4):
                    split(l, stage, q)
                    silu(l, stage, q)
                    if q >= 3:
                        hidden_hi(l, stage, q)
                with act.Fori(0, (N_UP - 5) // 2) as i:
                    for q in (4, 5):
                        split(l, stage, q, i)
                        silu(l, stage, q, i)
                        hidden_hi(l, stage, q, i)
                for q in range(N_UP - 1, FFN_STEPS):
                    split(l, stage, q)
                    if q - 2 < N_UP:
                        silu(l, stage, q)
                    if q - 3 < N_UP:
                        hidden_hi(l, stage, q)
                    if q == FFN_GROUPS_SPLIT + 2:
                        leave_first(l, stage, FFN_GROUPS_SPLIT)
                next_first(l, stage)
                leave(l, stage, FFN_STEPS - 1)

            def next_first(l, stage):
                if stage < 2:
                    split(l, stage + 1, 0)

            def enter_split(l, stage):
                enter(l, stage)
                split(l, stage, 1, quarters=range(4) if stage == 0 else (1, 2, 3))

            def mix(l):
                enter_split(l, 1)
                mmw = lambda q, seg, t: act.wait_ge(mm_done.sem, mm_done.at(l, mm_group(1, q, seg, t)))

                def gate(q, n):
                    br = next(b for b, s in BRANCH_STEPS.items() if 0 <= q - s < 3)
                    g = 8 + 4 * (3 - br) + n
                    for t in range(2):
                        mmw(q, 0, t)
                        if br < 3:
                            act.wait_ge(merged_done.sem, merged_done.at(l, 4 * (2 - br) + 2 * n + t + 1))
                        nc.scalar.activation(gates[:, t, n * 512:(n + 1) * 512], Z[pair_of(1, g)][t][:],
                                             ACT.Sigmoid).then_inc(gate_ready.sem, 1)

                def q_copy(n):
                    for t in range(2):
                        mmw(UQ, n, t)
                        w = (512, 256)[n]
                        copy(qf[:, t, 512 * n:512 * n + w], Z[pair_of(1, 4 + n)][t][:, 0:w]
                             ).then_inc(q_copied.sem, 1)

                def kv_copy(n):
                    for t in range(2):
                        mmw(UKV, n, t)
                        kv = Z[pair_of(1, 6 + n)][t][:].rearrange("p (h d) -> p h d", h=4)
                        copy(kf[:, t, :].rearrange("p (h d) -> p h d", h=H)[:, 4 * n:4 * n + 4, 0:NOPE],
                             kv[:, :, 0:NOPE])
                        copy(v[:, t, :].rearrange("p (h d) -> p h d", h=H)[:, 4 * n:4 * n + 4, :],
                             kv[:, :, NOPE:NOPE + VH]).then_inc(kv_copied.sem, 1)

                def exps(i):
                    act.wait_ge(nmx_ready.sem, nmx_ready.at(l, i + 1))
                    if i >= 1:
                        act.wait_ge(pT_filled.sem, pT_filled.at(l, 2 * i))
                    for h in range(4):
                        ins = nc.scalar.activation(p[:, h, :], T[2 + h // 2][:, (h % 2) * 256:(h % 2) * 256 + 256],
                                                   ACT.Exp, bias=nmx[:, h:h + 1], scale=QKD ** -0.5,
                                                   accum_out=rs[:, h:h + 1])
                    ins.then_inc(exp_done.sem, 1)

                def pT_copy(i):
                    act.wait_ge(pT_filled.sem, pT_filled.at(l, 2 * i + 1))
                    copy(pT[:, 0, :, :], T[0][:].rearrange("p (h n) -> p h n", h=4)).then_inc(pT_act.sem, 1)

                def o_copy(i):
                    act.wait_ge(o_done.sem, o_done.at(l, i + 1))
                    t, hh = i // 2, i % 2
                    copy(oT_hi[:, 2 * hh:2 * hh + 2, t * 128:(t + 1) * 128],
                         T[0][:, 0:256].rearrange("p (c n) -> p c n", c=2)).then_inc(o_hi.sem, 1)

                def m_copy(f):
                    act.wait_ge(m_filled.sem, m_filled.at(l, f + 1))
                    kh, t = f // 2, f % 2
                    copy(hT_hi[:, 4 * kh:4 * kh + 4, t * 128:(t + 1) * 128],
                         T[f][:].rearrange("p (k n) -> p k n", k=4)).then_inc(m_hi.sem, 1)

                def kq_copy(f):
                    act.wait_ge(kq_filled.sem, kq_filled.at(l, f + 1))
                    dst = kT if f < 4 else qT
                    t, hh = (f % 4) // 2, f % 2
                    bank = T[(2, 3, 0, 1)[f % 4]]
                    copy(dst[0:QKD, 4 * hh:4 * hh + 4, t * 128:(t + 1) * 128],
                         bank[0:QKD, :].rearrange("p (h n) -> p h n", h=4)).then_inc(kq_act.sem, 1)

                for q in range(2, MIX_STEPS):
                    if q == 15:
                        split(l, 1, q, quarters=(0,))
                        gate(q - 2, (q - 2) % 3)
                        pT_copy(2)
                        split(l, 1, q, quarters=(1, 2, 3))
                    elif q not in (2, 3, 4):
                        split(l, 1, q)
                    if q in (13, 17):
                        pT_copy((q - 11) // 2)
                    if q == 2:
                        for t in range(2):
                            mmw(0, 0, t)
                            za_bank = Z[pair_of(1, 0)][t]
                            copy(za[:, t, :], za_bank[:]).then_inc(za_copied.sem, 1)
                            nc.scalar.activation(junk[:, 512 * t:512 * t + QL], za_bank[:, 0:QL], ACT.Square,
                                                 accum_out=ssa[:, t, 0:1])
                            nc.scalar.activation(junk[:, 512 * t + QL:512 * t + 512 - ROPE],
                                                 za_bank[:, QL:QL + KVL], ACT.Square,
                                                 accum_out=ssa[:, t, 1:2]).then_inc(ssa_ready.sem, 1)
                        split(l, 1, q)
                    if q == 3:
                        for t in range(2):
                            mmw(1, 0, t)
                            nc.scalar.activation(u[:, t, :], Z[pair_of(1, 1)][t][:, CC:2 * CC], ACT.Sigmoid
                                                 ).then_inc(sgb_ready.sem, 1)
                        split(l, 1, q)
                    if q == 4:
                        act.wait_ge(an_filled.sem, an_filled.at(l, 2))
                        for k in range(4):
                            r = QL - 256 if k == 2 else 128
                            nc.scalar.activation(aT_hi[0:r, k, :], T[k // 2][0:r, (k % 2) * 256:(k % 2) * 256 + 256],
                                                 ACT.Copy, scale=vec[0:r, V_QG + k:V_QG + k + 1]
                                                 ).then_inc(a_hi.sem, 1)
                        split(l, 1, q)
                        for t in range(2):
                            mmw(2, 0, t)
                            copy(zt[:, t, 0, :], Z[pair_of(1, 2)][t][:]).then_inc(zt_copied.sem, 1)
                        act.wait_ge(u_filled.sem, u_filled.at(l, 1))
                        copy(uT[:, :, CW // 2:CW // 2 + S], T[2][:].rearrange("p (c n) -> p c n", c=2)
                             ).then_inc(uT_ready.sem, 1)
                    if q == 5:
                        for t in range(2):
                            mmw(3, 0, t)
                            copy(zt[:, t, 1, :], Z[pair_of(1, 3)][t][:]).then_inc(zt_copied.sem, 1)
                        act.wait_ge(pool1_done.sem, pool1_done.at(l, 1))
                        copy(dT[:, 0:2, :], T[0][:].rearrange("p (g n) -> p g n", g=2)).then_inc(dT_act.sem, 1)
                        q_copy(0)
                    if q == 6:
                        q_copy(1)
                        for g in (0, 2):
                            act.wait_ge(fnet1_done.sem, fnet1_done.at(l, g + 1))
                            copy(U[:, g, :], T[(2, 3, 0, 1)[g]][:]).then_inc(U_act.sem, 1)
                        kv_copy(0)
                    if q == 7:
                        kv_copy(1)
                    if q in (8, 9, 11, 12, 14, 17, 18):
                        gate(q - 2, (q - 2) % 3)
                    if q in (16,):
                        exps(3)
                    if q == 8:
                        act.wait_ge(fnet2_done.sem, fnet2_done.at(l, 2))
                        for b in range(2):
                            copy(bT_hi[:, 2 * b:2 * b + 2, :], T[b][:].rearrange("p (g n) -> p g n", g=2)
                                 ).then_inc(b_hi.sem, 1)
                        kq_copy(0)
                    if q == 9:
                        kq_copy(2)
                        kq_copy(4)
                    if q == 10:
                        kq_copy(6)
                        exps(0)
                    if q == 11:
                        act.wait_ge(pool2_done.sem, pool2_done.at(l, 2))
                        act.wait_ge(mm_done.sem, mm_done.at(l, mm_group(1, 8, 1, 1)))
                        for g in range(4):
                            ins = nc.scalar.activation(bT_hi[:, g, :], T[2 + g // 2][:, (g % 2) * 256:(g % 2) * 256 + 256],
                                                       ACT.Copy, scale=vec[:, V_PS + g:V_PS + g + 1])
                            if g % 2:
                                ins.then_inc(b_hi.sem, 1)
                        pT_copy(0)
                    if q == 12:
                        o_copy(0)
                        exps(1)
                    if q == 14:
                        act.wait_ge(lnx_filled.sem, lnx_filled.at(l, 1))
                        for k in range(2):
                            ins = nc.scalar.activation(sgv[:, k, :], T[1][:, k * 256:(k + 1) * 256], ACT.Sigmoid,
                                                       scale=vec[:, V_LG + k:V_LG + k + 1],
                                                       bias=vec[:, V_LB + k:V_LB + k + 1])
                        ins.then_inc(sgv_ready.sem, 1)
                        o_copy(1)
                        exps(2)
                        act.wait_ge(lnv_ready.sem, lnv_ready.at(l, 1))
                        act.wait_ge(mm_done.sem, mm_done.at(l, mm_group(1, 11, 1, 1)))
                        copy(bT_hi[:, 0:2, :], lnv[:, :, :]).then_inc(b_hi.sem, 1)
                    if q == 16:
                        o_copy(2)
                    if q == 17:
                        o_copy(3)
                    if q == 18:
                        for f in range(3):
                            m_copy(f)
                    if q == 19:
                        m_copy(3)
                leave_first(l, 1, 18)
                next_first(l, 1)
                leave(l, 1, 19)

            act.wait_ge(pro_arrived[2 * PRO_ORDER[-1]], 16)
            act.dma_start(dft[:, :, :], dft_c.rearrange("(k p) n -> p k n", p=128)).then_inc(consts_arrived, 16)
            act.dma_start(chan[:, :, :], chan_c.rearrange("p (k n) -> p k n", k=2)).then_inc(consts_arrived, 16)
            act.dma_start(band[:, :, :, :], band_c).then_inc(consts_arrived, 16)
            act.dma_start(rope[:, :, :, :], rope_c.rearrange("(t p) a b -> p t a b", p=128)
                          ).then_inc(consts_arrived, 16)
            with act.Fori(0, L) as l:
                ffn(l, 0)
                mix(l)
                ffn(l, 2)

        @block.vector
        def _(dve):
            tt = nc.vector.tensor_tensor
            stt = nc.vector.scalar_tensor_tensor
            tsc = nc.vector.tensor_scalar
            chain = dve_chain
            chain.per_layer = DVE_CHAIN_LAYER

            def split(l, stage, q, i=0, quarters=range(4)):
                panel, slot, _ = stage_panel(stage, q, i)
                for n in quarters:
                    parts, a, b = pieces(stage, q)[n]
                    dve.wait_ge(hi_done.sem, hi_done.at(l, 4 * panel + n + 1))
                    tt(w_lo[0:parts, slot, a:b], raw[0:parts, slot, a:b],
                       w_hi[0:parts, slot, a:b].bitcast(f32), ALU.subtract).then_inc(lo_done.sem, 1)

            def ada_step(l, stage, q, i=0):
                half = q // 2 + i
                if stage != 1:
                    half += 2 if q < 8 else -4
                elif q >= 8:
                    half = q // 2 - 4
                acc = modacc[:].rearrange("p h n -> p (h n)")[:, ds(half * 512, 512)]
                for e in range(2):
                    dve.wait_ge(ada_arrived[e].sem,
                                ada_arrived[e].at(l, 16 * (ADA_STEPS * stage + q + 2 * i + 1)))
                    for r in range(2):
                        j = 4 * (q % 2) + 2 * e + r
                        if j == 0:
                            ins = tsc(acc, ada[:, e, r, :], c_act[:, 0:1], None, ALU.mult)
                        else:
                            ins = stt(acc, ada[:, e, r, :], c_act[:, j:j + 1], acc, ALU.mult, ALU.add)
                        if r == 0:
                            chain.link(ins)
                        else:
                            ins.then_inc(ada_done.sem, 1)
                            dve.wait_ge(ada_done.sem,
                                        ada_done.at(l, 2 * (ADA_STEPS * stage + q + 2 * i) + e + 1))

            def normalise_x(l, stage, t):
                dve.wait_ge(rsx_ready.sem, rsx_ready.at(l, 2 * stage + t + 1))
                tsc(tmp[:, t, :], xs[:, t, :], rsx[:, t:t + 1], None, ALU.mult).then_inc(xn_ready.sem, 1)

            def modulation(l, stage, half):
                dve.wait_ge(cols_summed.sem, cols_summed.at(l, 2 * stage + half + 1))
                ks, sums = slice(4 * half, 4 * half + 4), T[2 + half]

                def col(first):
                    c0 = first + 8 * (stage % 3) + 4 * half
                    return vec[:, c0:c0 + 4]
                bias = V_B + 16 * (stage % 3)
                tt(ab[:, 0, ks], sums[:, 0:4], col(bias), ALU.add)
                chain.link(tt(ab[:, 1, ks], sums[:, 4:8], col(bias + 8), ALU.add))
                stt(ab[:, 2, ks], ab[:, 1, ks], 1.0, col(V_G), ALU.add, ALU.mult).then_inc(ab_ready.sem, 1)

            def enter(l, stage):
                def modulated(t):
                    dve.wait_ge(ht_filled.sem, ht_filled.at(l, 4 * stage + 2 * t + 2))
                    for k in range(4, 8):
                        ins = tsc(tmp[:, t, k * 128:(k + 1) * 128],
                                  T[2 * t + 1][:, (k - 4) * 128:(k - 3) * 128],
                                  ab[:, 2, k:k + 1], ab[:, 0, k:k + 1], ALU.mult, ALU.add)
                    ins.then_inc(hf_dve.sem, 1)

                def lo(t, half):
                    dve.wait_ge(ht_hi.sem, ht_hi.at(l, 4 * stage + 2 * t + half + 1))
                    sl = (slice(None), slice(4 * half, 4 * half + 4), slice(t * 128, (t + 1) * 128))
                    tt(hT_lo[sl], tmp[:, t, half * 512:(half + 1) * 512].rearrange("p (k n) -> p k n", k=4),
                       hT_hi[sl].bitcast(f32), ALU.subtract).then_inc(ht_lo.sem, 1)

                if stage == 0:
                    split(l, 0, 0, quarters=(0,))
                lo(0, 0)
                modulation(l, stage, 1)
                dve.wait_ge(ab_ready.sem, ab_ready.at(l, 2 * stage + 2))
                modulated(0)
                normalise_x(l, stage, 1)
                if stage == 0:
                    split(l, 0, 0, quarters=(1,))
                lo(0, 1)
                if stage == 0:
                    split(l, 0, 0, quarters=(2, 3))
                else:
                    split(l, stage, 1, quarters=(0,))
                modulated(1)
                lo(1, 0)
                lo(1, 1)

            def scaled_y(l, stage, n, t):
                dve.wait_ge(ssy_ready.sem, ssy_ready.at(l, 4 * stage + 2 * n + t + 1))
                g = (N_UP if stage != 1 else 24) + n
                tt(tmp[:, t, n * 512:(n + 1) * 512], Z[pair_of(stage, g)][t][:],
                   gain[:, n * 512:(n + 1) * 512], ALU.mult).then_inc(y_scaled.sem, 1)

            def leave(l, stage):
                for t in range(2):
                    scaled_y(l, stage, 1, t)
                    if t:
                        modulation(l, stage + 1, 0)
                    dve.wait_ge(y_scaled.sem, y_scaled.at(l, 4 * stage + 2 + t + 1))
                    dve.wait_ge(rsy_ready.sem, rsy_ready.at(l, 2 * stage + t + 1))
                    stt(xs[:, t, :], tmp[:, t, :], rsy[:, t:t + 1], xs[:, t, :], ALU.mult, ALU.add
                        ).then_inc(x_updated.sem, 1)
                    if t == 0:
                        normalise_x(l, stage + 1, 0)

            def make_gain(l, stage):
                dve.wait_ge(rows_arrived.sem, rows_arrived.at(l, 32 * stage + 32))
                for n in range(2):
                    dve.wait_ge(gain_summed.sem, gain_summed.at(l, 2 * stage + n + 1))
                    sl = slice(n * 512, (n + 1) * 512)
                    bank = (T[3], T[1]) if stage != 1 else (T[0], T[1])
                    tt(tmp[:, 0, sl], bank[n][:], tmp[:, 0, sl], ALU.add).then_inc(gain_read.sem, 1)
                dve.wait_ge(gain_read.sem, gain_read.at(l, 2 * stage + 2))
                chain.link(stt(gain[:], tmp[:, 0, :], 1.0 if stage == 1 else 0.5, gain[:], ALU.mult, ALU.mult))

            def gated_hidden(l, stage, q, i=0):
                base = 2 * N_UP * (stage // 2) + 2 * (q - 2) + 4 * i
                for t in range(2):
                    dve.wait_ge(silu_ready.sem, silu_ready.at(l, base + t + 1))
                    tt(hid[:, q % 2, t, :], hid[:, q % 2, t, :], Z[pair_of(stage, q)][t][:, UPW:2 * UPW],
                       ALU.mult).then_inc(hid_ready.sem, 1)

            def hidden_lo(l, stage, q, i=0):
                dve.wait_ge(hid_hi_ready.sem, hid_hi_ready.at(l, N_UP * (stage // 2) + q - 2 + 2 * i))
                at_ = (q - 3 + 2 * i) * 512
                tt(hid_lo[:, :, :].rearrange("p k n -> p (k n)")[:, ds(at_, 512)], T[(q - 3) % 2][:],
                   hid_hi[:, :, :].rearrange("p k n -> p (k n)")[:, ds(at_, 512)].bitcast(f32),
                   ALU.subtract).then_inc(hid_lo_ready.sem, 1)

            def ffn(l, stage):
                enter(l, stage)
                split(l, stage, 1, quarters=range(4) if stage == 0 else (1, 2, 3))
                for q in range(2, 4):
                    split(l, stage, q)
                    gated_hidden(l, stage, q)
                    if q >= 3:
                        hidden_lo(l, stage, q)
                    ada_step(l, stage, q - ADA_FIRST)
                before = chain.n
                pass_waits(dve, "dve")
                with dve.Fori(0, (N_UP - 5) // 2) as i:
                    chain.extra = i * LOOP_LINKS
                    for q in (4, 5):
                        split(l, stage, q, i)
                        gated_hidden(l, stage, q, i)
                        hidden_lo(l, stage, q, i)
                        ada_step(l, stage, q - ADA_FIRST, i)
                    assert chain.n - before == LOOP_LINKS, chain.n - before
                chain.extra = 0
                chain.n = before + LOOP_LINKS * ((N_UP - 5) // 2)
                for q in range(N_UP - 1, FFN_STEPS):
                    split(l, stage, q)
                    if q - 2 < N_UP:
                        gated_hidden(l, stage, q)
                    if q - 3 < N_UP:
                        hidden_lo(l, stage, q)
                    if q < ADA_STEPS + ADA_FIRST:
                        ada_step(l, stage, q - ADA_FIRST)
                    if q == FFN_GROUPS_SPLIT + 1:
                        make_gain(l, stage)
                    if q == FFN_GROUPS_SPLIT + 2:
                        for t in range(2):
                            scaled_y(l, stage, 0, t)
                if stage < 2:
                    split(l, stage + 1, 0)
                else:
                    nc.vector.tensor_copy(vec[:], vec_next[:, ds(l * NVC, NVC)]).then_inc(vec_ready.sem, 1)
                    dve.wait_ge(vec_ready.sem, vec_ready.at(l, 1))
                leave(l, stage)

            def mix(l):
                enter(l, 1)
                split(l, 1, 1, quarters=(1, 2, 3))
                ada_step(l, 1, 0)

                def merge(q, n, tiles=range(2)):
                    br = next(b for b, s in BRANCH_STEPS.items() if 0 <= q - s < 3)
                    g = 8 + 4 * (3 - br) + 2 + n
                    for t in tiles:
                        dve.wait_ge(gate_ready.sem, gate_ready.at(l, 4 * (3 - br) + 2 * n + t + 1))
                        dve.wait_ge(mm_done.sem, mm_done.at(l, mm_group(1, q, n, t)))
                        sl = slice(n * 512, (n + 1) * 512)
                        if br == 3:
                            tt(tmp[:, t, sl], gates[:, t, sl], Z[pair_of(1, g)][t][:], ALU.mult
                               ).then_inc(merged_done.sem, 1)
                        else:
                            chain.link(tt(gates[:, t, sl], gates[:, t, sl], Z[pair_of(1, g)][t][:], ALU.mult))
                            tt(tmp[:, t, sl], tmp[:, t, sl], gates[:, t, sl], ALU.add
                               ).then_inc(merged_done.sem, 1)

                def conv_taps(first, last):
                    for tap in range(first, last):
                        for k in range(2):
                            w = vec[:, V_CW + 2 * tap + k:V_CW + 2 * tap + k + 1]
                            src = uT[:, k, tap:tap + S]
                            if tap == 0:
                                ins = tsc(yc[:, k, :], src, w, vec[:, V_CB + k:V_CB + k + 1], ALU.mult, ALU.add)
                            else:
                                ins = stt(yc[:, k, :], src, w, yc[:, k, :], ALU.mult, ALU.add)
                        if tap == CW - 1:
                            ins.then_inc(yc_ready.sem, 1)
                        else:
                            chain.link(ins)

                def row_max(i):
                    for b in range(2):
                        dve.wait_ge(scores_done.sem, scores_done.at(l, 2 * i + b + 1))
                        ins = nc.vector.reduce_max(mx[:, 2 * b:2 * b + 2],
                                                   T[2 + b][:].rearrange("p (h n) -> p h n", h=2), axis=AX.X)
                    chain.link(ins)
                    tsc(nmx[:], mx[:], -(QKD ** -0.5), None, ALU.mult).then_inc(nmx_ready.sem, 1)

                def normalise(i):
                    dve.wait_ge(exp_done.sem, exp_done.at(l, i + 1))
                    chain.link(nc.vector.reciprocal(rinv[:], rs[:]))
                    tt(p[:, :, :], p[:, :, :], rinv[:].unsqueeze(2).to_broadcast([128, 4, S]), ALU.mult
                       ).then_inc(p_ready.sem, 1)

                def pT_copy(i):
                    dve.wait_ge(pT_filled.sem, pT_filled.at(l, 2 * i + 2))
                    nc.vector.tensor_copy(pT[:, 1, :, :], T[1][:].rearrange("p (h n) -> p h n", h=4)
                                          ).then_inc(pT_dve.sem, 1)

                def o_rest(i):
                    t, hh = i // 2, i % 2
                    dve.wait_ge(o_hi.sem, o_hi.at(l, i + 1))
                    sl = (slice(None), slice(2 * hh, 2 * hh + 2), slice(t * 128, (t + 1) * 128))
                    tt(oT_lo[sl], T[0][:, 0:256].rearrange("p (c n) -> p c n", c=2), oT_hi[sl].bitcast(f32),
                       ALU.subtract).then_inc(o_lo.sem, 1)

                def kq_copy(f):
                    dve.wait_ge(kq_filled.sem, kq_filled.at(l, f + 1))
                    dst = kT if f < 4 else qT
                    t, hh = (f % 4) // 2, f % 2
                    bank = T[(2, 3, 0, 1)[f % 4]]
                    nc.vector.tensor_copy(dst[0:QKD, 4 * hh:4 * hh + 4, t * 128:(t + 1) * 128],
                                          bank[0:QKD, :].rearrange("p (h n) -> p h n", h=4)
                                          ).then_inc(kq_dve.sem, 1)

                for q in range(2, MIX_STEPS):
                    if q in (13, 15, 17):
                        pT_copy((q - 11) // 2)
                    if q in (14, 16):
                        row_max((q - 10) // 2)
                    if q == 19:
                        split(l, 1, q, quarters=(0, 1))
                        m_rest(l, 3)
                        split(l, 1, q, quarters=(2, 3))
                    elif q not in (3, 4):
                        split(l, 1, q)
                    if q == 2:
                        for t in range(2):
                            dve.wait_ge(rsa_ready.sem, rsa_ready.at(l, t + 1))
                            tsc(za[:, t, 0:QL], za[:, t, 0:QL], rsa[:, t, 0:1], None, ALU.mult)
                            tsc(za[:, t, QL:QL + KVL], za[:, t, QL:QL + KVL], rsa[:, t, 1:2], None, ALU.mult
                                ).then_inc(an_ready.sem, 1)
                        for side in (slice(0, CW // 2), slice(CW // 2 + S, PADW)):
                            ins = nc.vector.memset(uT[:, :, side], 0.0)
                        chain.link(ins)
                    if q == 3:
                        for t in range(2):
                            dve.wait_ge(sgb_ready.sem, sgb_ready.at(l, t + 1))
                            tt(u[:, t, :], u[:, t, :], Z[pair_of(1, 1)][t][:, 0:CC], ALU.mult
                               ).then_inc(u_ready.sem, 1)
                        split(l, 1, q)
                    if q == 4:
                        for k in range(4):
                            r = QL - 256 if k == 2 else 128
                            dve.wait_ge(a_hi.sem, a_hi.at(l, 2 * (k // 2) + 2))
                            stt(aT_lo[0:r, k, :], T[k // 2][0:r, (k % 2) * 256:(k % 2) * 256 + 256],
                                vec[0:r, V_QG + k:V_QG + k + 1], aT_hi[0:r, k, :].bitcast(f32),
                                ALU.mult, ALU.subtract).then_inc(a_lo.sem, 1)
                        split(l, 1, q)
                        dve.wait_ge(uT_ready.sem, uT_ready.at(l, 1))
                        conv_taps(0, 4)
                    if q == 5:
                        dve.wait_ge(pool1_done.sem, pool1_done.at(l, 2))
                        nc.vector.tensor_copy(dT[:, 2:4, :], T[1][:].rearrange("p (g n) -> p g n", g=2)
                                              ).then_inc(dT_dve.sem, 1)
                        conv_taps(4, 9)
                    if q == 6:
                        for g in (1, 3):
                            dve.wait_ge(fnet1_done.sem, fnet1_done.at(l, g + 1))
                            nc.vector.tensor_copy(U[:, g, :], T[(2, 3, 0, 1)[g]][:]).then_inc(U_dve.sem, 1)
                        conv_taps(9, 14)
                    if q == 7:
                        make_gain(l, 1)
                        conv_taps(14, 20)
                    if q == 8:
                        dve.wait_ge(k_rotated.sem, k_rotated.at(l, 2))
                        for b in range(2):
                            dve.wait_ge(b_hi.sem, b_hi.at(l, b + 1))
                            tt(bT_lo[:, 2 * b:2 * b + 2, :], T[b][:].rearrange("p (g n) -> p g n", g=2),
                               bT_hi[:, 2 * b:2 * b + 2, :].bitcast(f32), ALU.subtract).then_inc(b_lo.sem, 1)
                        kq_copy(1)
                        conv_taps(20, 24)
                    if q == 9:
                        kq_copy(3)
                        kq_copy(5)
                        conv_taps(24, 27)
                        merge(8, 0)
                    if q == 10:
                        kq_copy(7)
                        row_max(0)
                        merge(8, 1)
                        normalise(0)
                        conv_taps(27, 31)
                    if q == 11:
                        for b in range(2):
                            dve.wait_ge(b_hi.sem, b_hi.at(l, 3 + b))
                            for g in (2 * b, 2 * b + 1):
                                ins = stt(bT_lo[:, g, :], T[2 + b][:, (g % 2) * 256:(g % 2) * 256 + 256],
                                          vec[:, V_PS + g:V_PS + g + 1], bT_hi[:, g, :].bitcast(f32),
                                          ALU.mult, ALU.subtract)
                            ins.then_inc(b_lo.sem, 1)
                        pT_copy(0)
                    if q == 12:
                        o_rest(0)
                        row_max(1)
                        dve.wait_ge(yc_filled.sem, yc_filled.at(l, 1))
                        for t in range(2):
                            ins = nc.vector.bn_stats(bns[:, t, :], T[1][:, t * 256:(t + 1) * 256])
                        chain.link(ins)
                        pass_waits(dve, "dve")
                        for t in range(2):
                            ins = nc.vector.bn_aggr(mv[:, t, :], bns[:, t, :])
                        ins.then_inc(mv_ready.sem, 1)
                        normalise(1)
                        dve.wait_ge(rsc_ready.sem, rsc_ready.at(l, 1))
                        for t in range(2):
                            ins = tsc(lnx[:, t, :], T[1][:, t * 256:(t + 1) * 256], mv[:, t, 0:1], rsc[:, t:t + 1],
                                      ALU.subtract, ALU.mult)
                        ins.then_inc(lnx_ready.sem, 1)
                        merge(11, 0)
                    if q == 13:
                        merge(11, 1)
                    if q == 14:
                        o_rest(1)
                        dve.wait_ge(sgv_ready.sem, sgv_ready.at(l, 1))
                        for k in range(2):
                            ins = tsc(lnv[:, k, :], T[1][:, k * 256:(k + 1) * 256], vec[:, V_LG + k:V_LG + k + 1],
                                      vec[:, V_LB + k:V_LB + k + 1], ALU.mult, ALU.add)
                        chain.link(ins)
                        tt(lnv[:, :, :], lnv[:, :, :], sgv[:, :, :], ALU.mult).then_inc(lnv_ready.sem, 1)
                        dve.wait_ge(b_hi.sem, b_hi.at(l, 5))
                        tt(bT_lo[:, 0:2, :], lnv[:, :, :], bT_hi[:, 0:2, :].bitcast(f32), ALU.subtract
                           ).then_inc(b_lo.sem, 1)
                        normalise(2)
                    if q == 15:
                        merge(14, 0)
                    if q == 16:
                        o_rest(2)
                        normalise(3)
                        merge(14, 1)
                    if q == 17:
                        o_rest(3)
                    if q == 18:
                        merge(17, 0)
                        merge(17, 1, tiles=(0,))
                        m_rest(l, 0)
                        merge(17, 1, tiles=(1,))
                        m_rest(l, 1)
                        m_rest(l, 2)
                    if q in MIX_ADA:
                        ada_step(l, 1, MIX_ADA.index(q))
                for t in range(2):
                    scaled_y(l, 1, 0, t)
                split(l, 2, 0)
                leave(l, 1)

            def m_rest(l, f):
                kh, t = f // 2, f % 2
                dve.wait_ge(m_hi.sem, m_hi.at(l, f + 1))
                sl = (slice(None), slice(4 * kh, 4 * kh + 4), slice(t * 128, (t + 1) * 128))
                tt(hT_lo[sl], T[f][:].rearrange("p (k n) -> p k n", k=4), hT_hi[sl].bitcast(f32),
                   ALU.subtract).then_inc(m_lo.sem, 1)

            nc.vector.memset(rows[:, :, :], 0.0).then_inc(rows_clear, 1)
            nc.vector.memset(ones[:], 1.0).then_inc(set_up, 1)
            dve.sem_inc(lo_done.sem, lo_done.credit)
            dve.sem_inc(ada_done.sem, ada_done.credit)
            dve.wait_ge(c_ready, 1)
            chain.start(dve, 0)
            chain.credit = 0
            for h in PRO_ORDER:
                for e in range(2):
                    dve.wait_ge(pro_arrived[2 * h + e], 16)
                    for r in range(4):
                        j = 4 * e + r
                        w = pro_ada[2 * h + e][:, r * 512:(r + 1) * 512]
                        acc = modacc[:, 2 + h, :]
                        if j == 0:
                            ins = tsc(acc, w, c_act[:, 0:1], None, ALU.mult)
                        else:
                            ins = stt(acc, w, c_act[:, j:j + 1], acc, ALU.mult, ALU.add)
                        if j < 7:
                            chain.link(ins)
                ins.then_inc(pro_done, 1)
                if h == PRO_ORDER[1]:
                    dve.wait_ge(pro_filled, 1)
                    for l0 in range(L):
                        src, n = Z[0][0][:, 256 * l0:256 * (l0 + 1)], (l0 - 1) % L * NVC
                        for dst in [vec_next[:, n:n + NVC]] + ([vec[:]] if l0 == 0 else []):
                            nc.vector.tensor_copy(dst[:, 0:NV], src[:, 0:NV])
                            ins = nc.vector.tensor_copy(dst[:, NV:NVC], src[:, 128:128 + 2 * CW])
                    chain.link(ins)
                if h == PRO_ORDER[2]:
                    modulation(0, 0, 0)
                    normalise_x(0, 0, 0)
                    dve.wait_ge(x_arrived[1], 16)
                    dve.sem_inc(x_updated.sem, x_updated.credit)
            chain.credit = chain.n
            with dve.Fori(0, L) as l:
                chain.start(dve, l)
                ffn(l, 0)
                mix(l)
                ffn(l, 2)
                assert chain.n == DVE_CHAIN_LAYER, chain.n

        @block.gpsimd
        def _(pool):
            tt = nc.gpsimd.tensor_tensor
            chain = pool_chain
            chain.per_layer = POOL_CHAIN_LAYER

            def rstd(out_ap, in_ap, width, cols, ready, more=()):
                pass_waits(pool, "pool")
                for o, i_, w in ((out_ap, in_ap, width),) + tuple(more):
                    ins = nc.gpsimd.tensor_scalar(o, i_, 1.0 / w, EPS, ALU.mult, ALU.add)
                chain.link(ins)
                whole, n = cols
                tt(whole, whole, minus_half[:, 0:n], ALU.pow).then_inc(ready.sem, 1)

            def rstd_of_x(l, stage, t):
                pool.wait_ge(ssx_ready.sem, ssx_ready.at(l, 2 * stage + t + 1))
                rstd(rsx[:, t:t + 1], ssx[:, t:t + 1], D, (rsx[:, t:t + 1], 1), rsx_ready)

            def leave(l, stage):
                for t in range(2):
                    pool.wait_ge(ssy_ready.sem, ssy_ready.at(l, 4 * stage + 2 + t + 1))
                    chain.link(tt(ssy[:, t, 0:1], ssy[:, t, 0:1], ssy[:, t, 1:2], ALU.add))
                    rstd(rsy[:, t:t + 1], ssy[:, t, 0:1], D, (rsy[:, t:t + 1], 1), rsy_ready)
                    if t == 0:
                        rstd_of_x(l, stage + 1, 0)

            def rotate(dst1, dst2, x1, x2, cos, sin, shape, ready, links):
                n = shape[0] * shape[1]
                view = lambda k: rot[:, k, 0:n].rearrange("p (h d) -> p h d", h=shape[0])
                tt(view(0), x1, cos, ALU.mult)
                tt(view(1), x2, sin, ALU.mult)
                tt(view(2), x1, sin, ALU.mult)
                chain.link(tt(view(3), x2, cos, ALU.mult))
                tt(dst1, view(0), view(1), ALU.subtract)
                ins = tt(dst2, view(2), view(3), ALU.add)
                if ready is None:
                    chain.link(ins)
                else:
                    ins.then_inc(ready.sem, 1)
                    pool.wait_ge(ready.sem, links)

            nc.gpsimd.memset(minus_half[:], -0.5).then_inc(set_up, 1)
            pool.wait_ge(set_up, 2)
            chain.start(pool, 0)
            rstd_of_x(0, 0, 0)
            chain.credit = chain.n
            with pool.Fori(0, L) as l:
                chain.start(pool, l)
                rstd_of_x(l, 0, 1)
                leave(l, 0)
                rstd_of_x(l, 1, 1)
                pool.wait_ge(consts_arrived, 64)
                for t in range(2):
                    pool.wait_ge(ssa_ready.sem, ssa_ready.at(l, t + 1))
                    rstd(rsa[:, t, 0:1], ssa[:, t, 0:1], QL, (rsa[:, t, :], 2), rsa_ready,
                         more=((rsa[:, t, 1:2], ssa[:, t, 1:2], KVL),))
                pool.wait_ge(q_copied.sem, q_copied.at(l, 4))
                for t in range(2):
                    heads = qf[:, t, :].rearrange("p (h d) -> p h d", h=H)
                    x1, x2 = heads[:, :, NOPE:NOPE + 16], heads[:, :, NOPE + 16:QKD]
                    cos = rope[:, t, 0, :].unsqueeze(1).to_broadcast([128, H, 16])
                    sin = rope[:, t, 1, :].unsqueeze(1).to_broadcast([128, H, 16])
                    rotate(x1, x2, x1, x2, cos, sin, (H, 16), q_rotated, q_rotated.at(l, t + 1))
                for t in range(2):
                    x1, x2 = za[:, t, QL + KVL:QL + KVL + 16], za[:, t, QL + KVL + 16:512]
                    one = lambda a: a.unsqueeze(1)
                    rotate(one(k_rot[:, t, 0:16]), one(k_rot[:, t, 16:32]), one(x1), one(x2),
                           one(rope[:, t, 0, :]), one(rope[:, t, 1, :]), (1, 16), None, None)
                    pass_waits(pool, "pool")
                    nc.gpsimd.tensor_copy(kf[:, t, :].rearrange("p (h d) -> p h d", h=H)[:, :, NOPE:QKD],
                                          k_rot[:, t, :].unsqueeze(1).to_broadcast([128, H, ROPE])
                                          ).then_inc(k_rotated.sem, 1)
                pool.wait_ge(mv_ready.sem, mv_ready.at(l, 1))
                pass_waits(pool, "pool")
                chain.link(nc.gpsimd.tensor_scalar(rsc[:], mv[:, :, 1], 1.0, EPS, ALU.mult, ALU.add))
                tt(rsc[:], rsc[:], minus_half[:, 0:2], ALU.pow).then_inc(rsc_ready.sem, 1)
                leave(l, 1)
                rstd_of_x(l, 2, 1)
                leave(l, 2)
                assert chain.n == POOL_CHAIN_LAYER, chain.n

        @block.tensor
        def _(pe):
            mm = nc.tensor.matmul

            def transpose(dst, src, rows_):
                return nc.tensor.transpose(dst, src, ident[0:rows_, 0:rows_])

            def product(l, stage, q, xh, xl, segs, i=0, before=None, between=None, operand=None):
                panel, slot, _ = stage_panel(stage, q, i)
                bounds = pieces(stage, q)
                seen = set()
                for s, (pair, blocks, width, starts, ends) in enumerate(segs):
                    for t in range(2):
                        if before is not None:
                            before(s, t)
                        for b, (k, col, parts) in enumerate(blocks):
                            if operand is not None:
                                operand(k, t)
                            last_piece = max(n for n, (_, a, e) in enumerate(bounds)
                                             if a < col + width and e > col)
                            if last_piece not in seen:
                                seen.add(last_piece)
                                pe.wait_ge(lo_done.sem, lo_done.at(l, 4 * panel + last_piece + 1))
                            z = Z[pair][t][:, 0:width]
                            a_hi_ = xh[0:parts, k, t * 128:(t + 1) * 128]
                            a_lo_ = xl[0:parts, k, t * 128:(t + 1) * 128]
                            wh = w_hi[0:parts, slot, col:col + width]
                            wl = w_lo[0:parts, slot, col:col + width]
                            mm(z, a_hi_, wh, start=starts and b == 0, stop=False)
                            mm(z, a_hi_, wl, start=False, stop=False)
                            ins = mm(z, a_lo_, wh, start=False, stop=ends and b == len(blocks) - 1)
                        ins.then_inc(mm_done.sem, 1)
                        if between is not None and s == 0 and t == 0:
                            between()

            def enter(l, stage, tiles=(0,)):
                for t in tiles:
                    pe.wait_ge(xn_ready.sem, xn_ready.at(l, 2 * stage + t + 1))
                    for half in range(2):
                        for k in range(4):
                            c0 = (4 * half + k) * 128
                            ins = transpose(T[2 * t + half][:, k * 128:(k + 1) * 128], tmp[:, t, c0:c0 + 128], 128)
                        ins.then_inc(ht_filled.sem, 1)

            def wide(stage, pair):
                return [(pair, [(k, 512 * k, 128) for k in range(KD)], 512, True, True)]

            def ht_wait(l, stage):
                seen = set()

                def wait(k, t):
                    n = 2 * t + k // 4
                    if n not in seen:
                        seen.add(n)
                        if n == 1:
                            pe.wait_ge(ab_ready.sem, ab_ready.at(l, 2 * stage + 2))
                            enter(l, stage, tiles=(1,))
                        pe.wait_ge(ht_lo.sem, ht_lo.at(l, 4 * stage + n + 1))
                return wait

            def hidden_fill(l, stage, q, i=0):
                if q >= 4:
                    pe.wait_ge(hid_lo_ready.sem, hid_lo_ready.at(l, N_UP * (stage // 2) + q - 3 + 2 * i))
                pe.wait_ge(hid_ready.sem, hid_ready.at(l, 2 * N_UP * (stage // 2) + 2 * (q - 1) + 4 * i))
                for ch in range(2):
                    for t in range(2):
                        ins = transpose(T[q % 2][:, ch * 256 + t * 128:ch * 256 + (t + 1) * 128],
                                        hid[:, q % 2, t, ch * 128:(ch + 1) * 128], 128)
                ins.then_inc(hid_filled.sem, 1)

            def sum_gain(l, stage, banks):
                pe.wait_ge(ada_done.sem, ada_done.at(l, 2 * ADA_STEPS * stage + (8 if stage == 1 else 24)))
                for n in range(2):
                    mm(banks[n][:], ones[:], modacc[:, n, :], start=True, stop=True).then_inc(gain_summed.sem, 1)

            def sum_cols(k_half, halves=(2, 3, 4, 5)):
                for n in range(8):
                    slot = halves[2 * (n // 4) + k_half]
                    ins = mm(T[2 + k_half][:, n:n + 1], modacc[:, slot, (n % 4) * 128:(n % 4 + 1) * 128],
                             ones[:, 0:1], start=True, stop=True)
                ins.then_inc(cols_summed.sem, 1)

            MIX_COLS = (2, 3, 0, 1)

            def ffn(l, stage):
                enter(l, stage)
                if stage == 0:
                    pe.wait_ge(pro_done, 4)
                sum_cols(1, halves=MIX_COLS if stage == 2 else (2, 3, 4, 5))
                first = ht_wait(l, stage)

                def up(q, i=0):
                    def bank_free(s, t):
                        if q >= 2:
                            pe.wait_ge(hid_ready.sem, hid_ready.at(
                                l, 2 * N_UP * (stage // 2) + 2 * (q - 2) + 4 * i + t + 1))
                    product(l, stage, q, hT_hi, hT_lo, wide(stage, pair_of(stage, q)), i=i, before=bank_free,
                            between=(lambda: hidden_fill(l, stage, q, i)) if q >= 2 else None,
                            operand=first if q < 2 else None)

                for q in range(4):
                    up(q)
                with pe.Fori(0, (N_UP - 5) // 2) as i:
                    for q in (4, 5):
                        up(q, i)
                up(N_UP - 1)
                for q in range(N_UP, FFN_STEPS):
                    blocks = down_blocks(q)
                    segs = []
                    for n in range(2):
                        mine = [(k, 512 * b, 128) for b, (bn, k) in enumerate(blocks) if bn == n]
                        if mine:
                            segs.append((pair_of(stage, N_UP + n), mine, 512, mine[0][0] == 0,
                                         mine[-1][0] == KF - 1))

                    def bank_free(s, t, q=q, blocks=blocks):
                        n = blocks[0][0] + s
                        if (q == N_UP and s == 0) or (q == FFN_GROUPS_SPLIT and s == 1):
                            up_panel = N_UP - 2 + n
                            pe.wait_ge(hid_ready.sem, hid_ready.at(
                                l, 2 * N_UP * (stage // 2) + 2 * up_panel + t + 1))
                    seen = set()

                    def ready(k, t, q=q, seen=seen):
                        if q <= FFN_GROUPS_SPLIT and k // 2 not in seen:
                            seen.add(k // 2)
                            pe.wait_ge(hid_lo_ready.sem, hid_lo_ready.at(l, N_UP * (stage // 2) + k // 2 + 1))
                    product(l, stage, q, hid_hi, hid_lo, segs, before=bank_free,
                            between=(lambda: hidden_fill(l, stage, q)) if q - 2 < N_UP else None, operand=ready)
                    if q == FFN_GROUPS_SPLIT:
                        sum_gain(l, stage, (T[3], T[1]))
                sum_cols(0)

            def mix(l):
                enter(l, 1)
                sum_cols(1)
                first = ht_wait(l, 1)
                w = lambda sig, n: pe.wait_ge(sig.sem, sig.at(l, n))

                def reader(g, t):
                    if g < 0:
                        return
                    if g == 0:
                        w(ssa_ready, t + 1)
                    elif g == 1:
                        w(u_ready, t + 1)
                    elif g < 4:
                        w(zt_copied, 2 * (g - 2) + t + 1)
                    elif g < 6:
                        w(q_copied, 2 * (g - 4) + t + 1)
                    elif g < 8:
                        w(kv_copied, 2 * (g - 6) + t + 1)
                    else:
                        br, part = (g - 8) // 4, (g - 8) % 4
                        if part < 2:
                            w(gate_ready, 4 * br + 2 * part + t + 1)
                        else:
                            w(merged_done, 4 * br + 2 * (part - 2) + t + 1)

                def whole(q, g, xh=hT_hi, xl=hT_lo, between=None, operand=None):
                    product(l, 1, q, xh, xl, wide(1, pair_of(1, g)), before=lambda s, t: reader(g - 2, t),
                            between=between, operand=operand)

                def scores(i):
                    t, hh = i // 2, i % 2
                    for b in range(2):
                        for h in (2 * b, 2 * b + 1):
                            head = 4 * hh + h
                            ins = mm(T[2 + b][:, (h % 2) * 256:(h % 2) * 256 + 256],
                                     qT[0:QKD, head, t * 128:(t + 1) * 128], kT[0:QKD, head, :],
                                     start=True, stop=True)
                        ins.then_inc(scores_done.sem, 1)

                def pT_fill(i):
                    w(p_ready, i + 1)
                    for kc in range(2):
                        for h in range(4):
                            ins = transpose(T[kc][:, h * 128:(h + 1) * 128], p[:, h, kc * 128:(kc + 1) * 128], 128)
                        ins.then_inc(pT_filled.sem, 1)

                def attend(i):
                    w(pT_act, i + 1)
                    w(pT_dve, i + 1)
                    hh = i % 2
                    for h in range(4):
                        head = 4 * hh + h
                        for kc in range(2):
                            ins = mm(T[0][64 * (h % 2):64 * (h % 2) + 64, (h // 2) * 128:(h // 2 + 1) * 128],
                                     v[:, kc, head * VH:(head + 1) * VH], pT[:, kc, h, :],
                                     start=kc == 0, stop=kc == 1)
                    ins.then_inc(o_done.sem, 1)

                def kq_fill(f):
                    src = kf if f < 4 else qf
                    t, hh = (f % 4) // 2, f % 2
                    bank = T[(2, 3, 0, 1)[f % 4]]
                    for h in range(4):
                        c0 = (4 * hh + h) * QKD
                        ins = transpose(bank[0:QKD, h * 128:(h + 1) * 128], src[:, t, c0:c0 + QKD], 128)
                    ins.then_inc(kq_filled.sem, 1)

                def m_fill(f):
                    kh, t = f // 2, f % 2
                    w(merged_done, 12 + f + 1)
                    for k in range(4):
                        c0 = (4 * kh + k) * 128
                        ins = transpose(T[f][:, k * 128:(k + 1) * 128], tmp[:, t, c0:c0 + 128], 128)
                    ins.then_inc(m_filled.sem, 1)

                def branch(q, g, rows_, between=None, before_last=None):
                    br = next(b for b, s in BRANCH_STEPS.items() if 0 <= q - s < 3)
                    segs = [(pair_of(1, g + n), [(k, k * D + n * 512, 128) for k in range(rows_)], 512, True, True)
                            for n in range(2)]

                    def before(s, t):
                        if before_last is not None and (s, t) == (1, 1):
                            before_last()
                        reader(g + s - 2, t)
                    product(l, 1, q, oT_hi if br == 0 else bT_hi, oT_lo if br == 0 else bT_lo, segs,
                            before=before, between=between)

                whole(0, 0, operand=first)
                whole(1, 1, operand=first)

                def latent_fill():
                    w(an_ready, 2)
                    for k in range(4):
                        r = QL - 256 if k == 2 else 128
                        c0 = 128 * k if k < 3 else QL
                        for t in range(2):
                            ins = transpose(T[k // 2][0:r, (k % 2) * 256 + t * 128:(k % 2) * 256 + (t + 1) * 128],
                                            za[:, t, c0:c0 + r], 128)
                        if k % 2:
                            ins.then_inc(an_filled.sem, 1)
                whole(2, 2, between=latent_fill)
                w(u_ready, 2)
                for k in range(2):
                    for t in range(2):
                        ins = transpose(T[2][:, k * 256 + t * 128:k * 256 + (t + 1) * 128],
                                        u[:, t, k * 128:(k + 1) * 128], 128)
                ins.then_inc(u_filled.sem, 1)
                whole(3, 3)
                pe.wait_ge(consts_arrived, 64)
                w(zt_copied, 2)
                w(a_lo, 4)
                for g in range(4):
                    bank, c0 = T[g // 2], (g % 2) * 256
                    z = lambda k: zt[:, k, 0, g * 128:(g + 1) * 128]
                    mm(bank[:, c0:c0 + BAND0], z(0), band[:, 0, g, 0:BAND0], start=True, stop=True)
                    mm(bank[:, c0 + BAND0:c0 + BAND], z(0), band[:, 0, g, BAND0:BAND], start=True, stop=False)
                    mm(bank[:, c0 + BAND0:c0 + BAND], z(1), band[:, 1, g, 0:BAND - BAND0], start=False, stop=True)
                    ins = mm(bank[:, c0 + BAND:c0 + S], z(1), band[:, 1, g, BAND - BAND0:BAND],
                             start=True, stop=True)
                    if g % 2:
                        ins.then_inc(pool1_done.sem, 1)
                w(a_lo, 4)
                uq_blocks = lambda c0: [(k, k * H * QKD + c0, 128 if k < 2 else QL - 256) for k in range(3)]
                product(l, 1, UQ, aT_hi, aT_lo,
                        [(pair_of(1, 4), uq_blocks(0), 512, True, True),
                         (pair_of(1, 5), uq_blocks(512), 256, True, True)],
                        before=lambda s, t: reader(2 + s, t))
                w(zt_copied, 4)
                w(uT_ready, 1)
                w(dT_act, 1)
                w(dT_dve, 1)
                for g in range(4):
                    for k in range(2):
                        ins = mm(T[(2, 3, 0, 1)[g]][:], zt[:, k, 1, g * 128:(g + 1) * 128], dft[:, k, :],
                                 start=k == 0, stop=k == 1)
                    ins.then_inc(fnet1_done.sem, 1)
                product(l, 1, UKV, aT_hi, aT_lo,
                        [(pair_of(1, 6 + n), [(3, 512 * n, 128)], 512, True, True) for n in range(2)],
                        before=lambda s, t: reader(4 + s, t))
                w(U_act, 2)
                w(U_dve, 2)
                sum_gain(l, 1, (T[0], T[1]))
                whole(6, 8)
                w(gain_read, 4)
                for b in range(2):
                    for k in range(2):
                        ins = mm(T[b][:].rearrange("p (g n) -> p g n", g=2), chan[:, k, :],
                                 U[:, 2 * b:2 * b + 2, k * 256:(k + 1) * 256], start=k == 0, stop=k == 1)
                    ins.then_inc(fnet2_done.sem, 1)
                w(kv_copied, 4)
                w(k_rotated, 2)
                kq_fill(0)
                kq_fill(1)
                whole(7, 9)
                w(b_lo, 2)
                kq_fill(2)
                kq_fill(3)
                w(q_rotated, 2)
                w(kq_act, 1)
                w(kq_dve, 1)
                kq_fill(4)
                kq_fill(5)
                branch(8, 10, 4)
                w(kq_act, 3)
                w(kq_dve, 3)
                kq_fill(6)
                kq_fill(7)
                scores(0)
                whole(9, 12)
                w(kq_act, 4)
                w(kq_dve, 4)
                pT_fill(0)
                w(poolw_arrived, 16)
                w(exp_done, 1)
                for g in range(4):
                    ins = mm(T[2 + g // 2][:, (g % 2) * 256:(g % 2) * 256 + 256], poolw[:, g, :], dT[:, g, :],
                             start=True, stop=True)
                    if g % 2:
                        ins.then_inc(pool2_done.sem, 1)
                whole(10, 13)
                attend(0)
                w(b_lo, 4)
                scores(1)
                w(yc_ready, 1)
                for k in range(2):
                    for t in range(2):
                        ins = transpose(T[1][:, t * 256 + k * 128:t * 256 + (k + 1) * 128],
                                        yc[:, k, t * 128:(t + 1) * 128], 128)
                ins.then_inc(yc_filled.sem, 1)
                branch(11, 14, 4)
                w(o_lo, 1)
                w(lnx_ready, 1)
                pT_fill(1)
                whole(12, 16)
                attend(1)
                w(lnx_ready, 1)
                for t in range(2):
                    for k in range(2):
                        ins = transpose(T[1][:, k * 256 + t * 128:k * 256 + (t + 1) * 128],
                                        lnx[:, t, k * 128:(k + 1) * 128], 128)
                ins.then_inc(lnx_filled.sem, 1)
                w(exp_done, 2)
                scores(2)
                whole(13, 17)
                w(o_lo, 2)
                w(lnv_ready, 1)
                pT_fill(2)
                w(b_lo, 5)
                branch(14, 18, 2)
                attend(2)
                w(exp_done, 3)
                scores(3)
                whole(15, 20)
                w(o_lo, 3)
                pT_fill(3)
                whole(16, 21, between=lambda: attend(3))
                w(o_lo, 4)
                branch(17, 22, 4, before_last=lambda: (m_fill(0), m_fill(1)))
                m_fill(2)
                seen = set()

                def merged_ready(k, t):
                    n = 2 * (k // 4) + t
                    if n not in seen:
                        seen.add(n)
                        w(m_lo, n + 1)
                whole(18, 24, operand=merged_ready, between=lambda: m_fill(3))
                whole(19, 25)
                pe.wait_ge(ada_done.sem, ada_done.at(l, 4 * ADA_STEPS))
                sum_cols(0, halves=MIX_COLS)

            pe.wait_ge(vrows_arrived, 12 * 16)
            pe.wait_ge(ident_arrived, 16)
            pe.wait_ge(set_up, 2)
            for l0 in range(L):
                transpose(Z[0][0][:, 256 * l0:256 * l0 + NV], rows[0:NV, l0, :], NV)
                ins = transpose(Z[0][0][:, 256 * l0 + 128:256 * l0 + 128 + 2 * CW], crows[:, l0, :], 2 * CW)
            ins.then_inc(pro_filled, 1)
            pe.wait_ge(pro_done, 2)
            sum_cols(0)
            pe.sem_inc(mm_done.sem, mm_done.credit)
            with pe.Fori(0, L) as l:
                ffn(l, 0)
                mix(l)
                ffn(l, 2)


DVE_CHAIN_LAYER = 134
POOL_CHAIN_LAYER = 27
LOOP_LINKS = 4

_INS = ["x", "c", "ada_w", "ada_b", "norm_g", "ffn1_w_in", "ffn1_w_out", "ffn2_w_in", "ffn2_w_out",
        "w_in", "q_norm_g", "w_uq", "kv_norm_g", "w_ukv", "w_a", "conv_w", "conv_b", "conv_ln_g",
        "conv_ln_b", "w_b", "pool_w", "pool_scale", "w_c", "w_d", "w_out"]


def shape_constants():
    import numpy as np

    ident = np.eye(128, dtype=np.float32)
    t = np.arange(S)
    angle = 2 * np.pi * np.outer(t, t) / S
    norm = (S * 128) ** -0.5
    dft = np.concatenate([np.cos(angle), np.sin(angle)], axis=1) * norm
    ch = np.arange(128)
    angle = 2 * np.pi * np.outer(ch, ch) / 128
    chan = np.concatenate([np.cos(angle), -np.sin(angle)], axis=1)
    full = np.zeros((len(WINDOWS), S, S))
    for g, w in enumerate(WINDOWS):
        lo = w // 2
        for s in range(S):
            a, b = max(s - lo, 0), min(s + w - lo, S)
            full[g, a:b, s] = 1.0 / (b - a)
            full[g, s, s] -= 1.0
    band = np.zeros((128, 2, len(WINDOWS), BAND))
    for g in range(len(WINDOWS)):
        band[:, 0, g, :] = full[g, 0:128, 0:BAND]
        band[:, 1, g, :] = full[g, 128:256, BAND0:S]
    inv = np.float32(10000.0) ** (-np.arange(0, ROPE, 2, dtype=np.float32) / np.float32(ROPE))
    ang = (t.astype(np.float32)[:, None] * inv[None, :]).astype(np.float64)
    rope = np.stack([np.cos(ang), np.sin(ang)], axis=1)
    return [("ident_c", ident), ("dft_c", dft), ("chan_c", chan), ("band_c", band), ("rope_c", rope)]


def kernel(**inputs):
    import numpy as np
    import concourse.bacc as bacc
    from concourse.bass_utils import run_bass_kernel_spmd

    nc = bacc.Bacc("TRN2", target_bir_lowering=False, num_devices=1, dynamic_dma_scratch_size=256)
    arrays, args = {}, []
    named = [(n, np.ascontiguousarray(inputs[n])) for n in _INS]
    named += [(n, np.ascontiguousarray(a, dtype=np.float32)) for n, a in shape_constants()]
    for name, a in named:
        arrays[f"in_{name}"] = a
        args.append(nc.dram_tensor(f"in_{name}", a.shape, mybir.dt.from_np(a.dtype), kind="ExternalInput").ap())
    args.append(nc.dram_tensor("out_0", (1, S, D), mybir.dt.float32, kind="ExternalOutput").ap())
    build(nc, *args)
    r = run_bass_kernel_spmd(nc, [arrays], core_ids=[0])
    return r.results[0]["out_0"]
```
